# Optimizing a Trainium2 kernel written in Bass

```python
import jax, jax.numpy as jnp
from jax import lax
import numpy as np
import math

D_MODEL = 1024
BATCH = 1
SEQ = 256
DEPTH = 1

HEAD_DIM = 64
DIL_PAIRS = ((128, 1), (512, 4), (2048, 16))
DIL_HEADS_PER_GROUP = 4
DIL_HEADS = DIL_HEADS_PER_GROUP * len(DIL_PAIRS)
DIL_WIDTH = DIL_HEADS * HEAD_DIM
DIL_OUT_WIDTH = DIL_HEADS_PER_GROUP * HEAD_DIM
SWA_WINDOW = 128
SWA_Q_HEADS = 8
SWA_KV_HEADS = 2
SWA_Q_WIDTH = SWA_Q_HEADS * HEAD_DIM
SWA_KV_WIDTH = SWA_KV_HEADS * HEAD_DIM
ROPE_THETA = 500000.0
ROPE_DIM = HEAD_DIM // 4
D_FF = 4 * D_MODEL
BLOCK = 128
EPS = 1e-6
NEG = -1e30
IN_SIZES = (DIL_WIDTH, DIL_WIDTH, DIL_WIDTH, SWA_Q_WIDTH, SWA_KV_WIDTH, SWA_KV_WIDTH, D_MODEL, D_MODEL)
IN_WIDTH = sum(IN_SIZES)


def rmsnorm(x, g):
    xf = x.astype(jnp.float32)
    y = xf * lax.rsqrt(jnp.mean(xf * xf, axis=-1, keepdims=True) + EPS)
    return (y * g.astype(jnp.float32)).astype(x.dtype)

def rope_tables(positions):
    inv_freq = ROPE_THETA ** (-jnp.arange(0, ROPE_DIM, 2, dtype=jnp.float32) / ROPE_DIM)
    ang = positions.astype(jnp.float32)[..., None] * inv_freq
    return jnp.cos(ang)[:, :, None, :], jnp.sin(ang)[:, :, None, :]

def apply_partial_rope(x, cos, sin):
    half = ROPE_DIM // 2
    xr = x[..., :ROPE_DIM].astype(jnp.float32)
    x1, x2 = xr[..., :half], xr[..., half:]
    rot = jnp.concatenate([x1 * cos - x2 * sin, x2 * cos + x1 * sin], axis=-1).astype(x.dtype)
    return jnp.concatenate([rot, x[..., ROPE_DIM:]], axis=-1)

def banded_attention(q, k, v, max_dist, sinks=None):
    B, N, L, H, Dh = q.shape
    Hkv = k.shape[3]
    G = H // Hkv
    Lp = -(-L // BLOCK) * BLOCK
    pad = Lp - L
    if pad:
        cfg = ((0, 0), (0, 0), (0, pad), (0, 0), (0, 0))
        q, k, v = jnp.pad(q, cfg), jnp.pad(k, cfg), jnp.pad(v, cfg)
    nb = Lp // BLOCK
    qb = q.reshape(B, N, nb, BLOCK, Hkv, G, Dh).astype(jnp.float32)

    def band(t):
        tp = jnp.pad(t, ((0, 0), (0, 0), (BLOCK, 0), (0, 0), (0, 0)))
        tb = tp.reshape(B, N, nb + 1, BLOCK, Hkv, Dh)
        return jnp.concatenate([tb[:, :, :-1], tb[:, :, 1:]], axis=3)

    kb = band(k).astype(jnp.float32)
    vb = band(v).astype(jnp.float32)
    scale = 1.0 / np.sqrt(Dh).astype(np.float32)
    s = jnp.einsum('bnjqhgd,bnjkhd->bnjhgqk', qb, kb) * scale
    blk = jnp.arange(nb)[:, None, None]
    qpos = blk * BLOCK + jnp.arange(BLOCK)[None, :, None]
    kpos = (blk - 1) * BLOCK + jnp.arange(2 * BLOCK)[None, None, :]
    dist = qpos - kpos
    mask = (dist >= 0) & (dist <= max_dist) & (kpos >= 0)
    s = jnp.where(mask[:, None, None, :, :], s, jnp.float32(NEG))
    m = jnp.max(s, axis=-1, keepdims=True)
    if sinks is not None:
        sk = sinks.astype(jnp.float32).reshape(Hkv, G)[:, :, None, None]
        m = jnp.maximum(m, sk)
        p = jnp.exp(s - m)
        denom = jnp.sum(p, axis=-1, keepdims=True) + jnp.exp(sk - m)
    else:
        p = jnp.exp(s - m)
        denom = jnp.sum(p, axis=-1, keepdims=True)
    o = jnp.einsum('bnjhgqk,bnjkhd->bnjqhgd', p / denom, vb)
    o = o.reshape(B, N, Lp, H, Dh)[:, :, :L].astype(v.dtype)
    lse = (m + jnp.log(denom))[..., 0]
    lse = lse.transpose(0, 1, 2, 5, 3, 4).reshape(B, N, Lp, H)[:, :, :L]
    return o, lse

def dilated_attention(q, k, v):
    B, S, _, Dh = q.shape
    outs, lses = [], []
    for g, (w, d) in enumerate(DIL_PAIRS):
        lo, hi = g * DIL_HEADS_PER_GROUP, (g + 1) * DIL_HEADS_PER_GROUP

        def strided(t):
            return t[:, :, lo:hi].reshape(B, S // d, d, DIL_HEADS_PER_GROUP, Dh).transpose(0, 2, 1, 3, 4)

        o, lse = banded_attention(strided(q), strided(k), strided(v), w // d)
        outs.append(o.transpose(0, 2, 1, 3, 4).reshape(B, S, DIL_HEADS_PER_GROUP, Dh))
        lses.append(lse.transpose(0, 2, 1, 3).reshape(B, S, DIL_HEADS_PER_GROUP))
    alpha = jax.nn.softmax(jnp.stack(lses, axis=0), axis=0)
    o = jnp.sum(alpha[..., None] * jnp.stack(outs, axis=0).astype(jnp.float32), axis=0)
    return o.reshape(B, S, DIL_OUT_WIDTH).astype(q.dtype)

def first_inputs(seed: int = 0) -> dict:
    key = jax.random.key(seed)
    ks = jax.random.split(key, 16)
    f32 = jnp.float32

    def w(k, shape, fan_in):
        return jax.random.normal(k, shape, f32) * (fan_in ** -0.5)

    def gain(k, shape):
        return 1.0 + 0.02 * jax.random.normal(k, shape, f32)

    x = jax.random.normal(ks[0], (BATCH, SEQ, D_MODEL), f32)
    offset = jax.random.randint(ks[1], (BATCH, 1), 0, 1024, dtype=jnp.int32)
    positions = (offset + jnp.arange(SEQ, dtype=jnp.int32)[None, :]).astype(jnp.int32)
    return {
        "x": x,
        "positions": positions,
        "ln1_g": gain(ks[2], (DEPTH, D_MODEL)),
        "w_in": w(ks[3], (DEPTH, D_MODEL, IN_WIDTH), D_MODEL),
        "q_norm_a": gain(ks[4], (DEPTH, HEAD_DIM)),
        "k_norm_a": gain(ks[5], (DEPTH, HEAD_DIM)),
        "q_norm_b": gain(ks[6], (DEPTH, HEAD_DIM)),
        "k_norm_b": gain(ks[7], (DEPTH, HEAD_DIM)),
        "sinks": 0.5 * jax.random.normal(ks[8], (DEPTH, SWA_Q_HEADS), f32),
        "w_branch_a": w(ks[9], (DEPTH, DIL_OUT_WIDTH, D_MODEL), DIL_OUT_WIDTH),
        "w_branch_b": w(ks[10], (DEPTH, SWA_Q_WIDTH, D_MODEL), SWA_Q_WIDTH),
        "w_out": w(ks[11], (DEPTH, D_MODEL, D_MODEL), D_MODEL),
        "ln2_g": gain(ks[12], (DEPTH, D_MODEL)),
        "w_up": w(ks[13], (DEPTH, D_MODEL, D_FF), D_MODEL),
        "w_down": w(ks[14], (DEPTH, D_FF, D_MODEL), D_FF),
    }

def first_block(x, positions, ln1_g, w_in, q_norm_a, k_norm_a, q_norm_b, k_norm_b, sinks,
              w_branch_a, w_branch_b, w_out, ln2_g, w_up, w_down):
    B, S, _ = x.shape
    cos, sin = rope_tables(positions)
    offsets = np.cumsum(np.array(IN_SIZES))[:-1].tolist()
    for l in range(DEPTH):
        h = rmsnorm(x, ln1_g[l])
        proj = h @ w_in[l]
        qa, ka, va, qb, kb, vb, ga, gb = jnp.split(proj, offsets, axis=-1)
        qa = apply_partial_rope(rmsnorm(qa.reshape(B, S, DIL_HEADS, HEAD_DIM), q_norm_a[l]), cos, sin)
        ka = apply_partial_rope(rmsnorm(ka.reshape(B, S, DIL_HEADS, HEAD_DIM), k_norm_a[l]), cos, sin)
        va = va.reshape(B, S, DIL_HEADS, HEAD_DIM)
        oa = dilated_attention(qa, ka, va)
        qb = apply_partial_rope(rmsnorm(qb.reshape(B, S, SWA_Q_HEADS, HEAD_DIM), q_norm_b[l]), cos, sin)
        kb = apply_partial_rope(rmsnorm(kb.reshape(B, S, SWA_KV_HEADS, HEAD_DIM), k_norm_b[l]), cos, sin)
        vb = vb.reshape(B, S, SWA_KV_HEADS, HEAD_DIM)
        ob, _ = banded_attention(qb[:, None], kb[:, None], vb[:, None], SWA_WINDOW - 1, sinks[l])
        ob = ob.reshape(B, S, SWA_Q_WIDTH)
        mix = jax.nn.sigmoid(ga) * (oa @ w_branch_a[l]) + jax.nn.sigmoid(gb) * (ob @ w_branch_b[l])
        x = x + mix @ w_out[l]
        h2 = rmsnorm(x, ln2_g[l])
        x = x + jnp.square(jax.nn.relu(h2 @ w_up[l])) @ w_down[l]
    return x


DEPTH_2 = 2

MIX_WIDTH = D_MODEL
DIFF_WIDTH = MIX_WIDTH // 2
DIFF_HEADS = DIFF_WIDTH // (2 * HEAD_DIM)
SWA_WIDTH = MIX_WIDTH - DIFF_WIDTH
SWA_Q_HEADS_2 = SWA_WIDTH // HEAD_DIM
SWA_GROUP = SWA_Q_HEADS_2 // SWA_KV_HEADS
WINDOW = 128
D_FF_2 = ((8 * D_MODEL // 3 + 127) // 128) * 128
ROPE_THETA_2 = 10000.0
ALPHA = (2.0 * DEPTH_2) ** 0.25
BETA = (8.0 * DEPTH_2) ** -0.25
LN_EPS = 1e-5
RMS_EPS = 1e-5

DQ = DIFF_HEADS * 2 * HEAD_DIM
DK = DIFF_HEADS * 2 * HEAD_DIM
DV = DIFF_HEADS * 2 * HEAD_DIM
SQ = SWA_Q_HEADS_2 * HEAD_DIM
SK = SWA_KV_HEADS * HEAD_DIM
SV = SWA_KV_HEADS * HEAD_DIM
IN_COLS = DQ + DK + DV + SQ + SK + SV


def layer_norm(x, g, b):
    xf = x.astype(jnp.float32)
    mu = jnp.mean(xf, axis=-1, keepdims=True)
    var = jnp.mean(jnp.square(xf - mu), axis=-1, keepdims=True)
    y = (xf - mu) * lax.rsqrt(var + LN_EPS) * g.astype(jnp.float32) + b.astype(jnp.float32)
    return y.astype(x.dtype)

def swiglu(x, w_in, w_out):
    h = x @ w_in
    gate, up = h[..., :D_FF_2], h[..., D_FF_2:]
    return (jax.nn.silu(gate) * up) @ w_out

def rope_tables_2(positions):
    inv = jnp.power(ROPE_THETA_2, -jnp.arange(0, HEAD_DIM, 2, dtype=jnp.float32) / HEAD_DIM)
    ang = positions.astype(jnp.float32)[..., None] * inv
    ang = jnp.concatenate([ang, ang], axis=-1)[:, :, None, :]
    return jnp.cos(ang), jnp.sin(ang)

def apply_rope(t, cos, sin):
    half = HEAD_DIM // 2
    t1, t2 = t[..., :half], t[..., half:]
    rot = jnp.concatenate([-t2, t1], axis=-1)
    return (t * cos.astype(t.dtype) + rot * sin.astype(t.dtype)).astype(t.dtype)

def diff_attention(q, k, v, lam, subln_g, lambda_init):
    B, S = q.shape[0], q.shape[1]
    nb = S // BLOCK
    scale = HEAD_DIM ** -0.5
    qb = q.reshape(B, nb, BLOCK, DIFF_HEADS, 2, HEAD_DIM).transpose(1, 0, 2, 3, 4, 5)

    def one_block(q_blk):
        s = jnp.einsum('bqhcd,bkhcd->bhcqk', q_blk, k).astype(jnp.float32) * scale
        p = jax.nn.softmax(s, axis=-1)
        a = p[:, :, 0] - lam * p[:, :, 1]
        return jnp.einsum('bhqk,bkhe->bqhe', a.astype(v.dtype), v)

    o = lax.map(one_block, qb)
    o = o.transpose(1, 0, 2, 3, 4).reshape(B, S, DIFF_HEADS, 2 * HEAD_DIM)
    of = o.astype(jnp.float32)
    of = of * lax.rsqrt(jnp.mean(jnp.square(of), axis=-1, keepdims=True) + RMS_EPS)
    of = of * subln_g.astype(jnp.float32) * (1.0 - lambda_init)
    return of.astype(v.dtype).reshape(B, S, DIFF_WIDTH)

def band_mask(S):
    nb = S // BLOCK
    qpos = jnp.arange(nb)[:, None, None] * BLOCK + jnp.arange(BLOCK)[None, :, None]
    kpos = (jnp.arange(nb)[:, None, None] - 1) * BLOCK + jnp.arange(3 * BLOCK)[None, None, :]
    return (jnp.abs(qpos - kpos) <= WINDOW) & (kpos >= 0) & (kpos < S)

def swa_sink_attention(q, k, v, sink, mask):
    B, S = q.shape[0], q.shape[1]
    nb = S // BLOCK
    scale = HEAD_DIM ** -0.5
    qb = q.reshape(B, nb, BLOCK, SWA_KV_HEADS, SWA_GROUP, HEAD_DIM)

    def band(t):
        tp = jnp.pad(t, ((0, 0), (BLOCK, BLOCK), (0, 0), (0, 0)))
        tp = tp.reshape(B, nb + 2, BLOCK, SWA_KV_HEADS, HEAD_DIM)
        return jnp.concatenate([tp[:, :-2], tp[:, 1:-1], tp[:, 2:]], axis=2)

    kb, vb = band(k), band(v)
    s = jnp.einsum('bnqhgd,bnkhd->bnhgqk', qb, kb).astype(jnp.float32) * scale
    s = jnp.where(mask[None, :, None, None, :, :], s, -jnp.inf)
    sk = sink.astype(jnp.float32).reshape(1, 1, SWA_KV_HEADS, SWA_GROUP, 1, 1)
    m = jnp.maximum(jnp.max(s, axis=-1, keepdims=True), sk)
    e = jnp.exp(s - m)
    p = e / (jnp.sum(e, axis=-1, keepdims=True) + jnp.exp(sk - m))
    o = jnp.einsum('bnhgqk,bnkhd->bnqhgd', p.astype(v.dtype), vb)
    return o.reshape(B, S, SWA_WIDTH)

def hybrid_mixer(x, cos, sin, mask, w_in, w_out, lam_vec, subln_g, sink, lambda_init):
    B, S = x.shape[0], x.shape[1]
    h = x @ w_in
    o0 = 0
    dq = h[..., o0:o0 + DQ]; o0 += DQ
    dk = h[..., o0:o0 + DK]; o0 += DK
    dv = h[..., o0:o0 + DV]; o0 += DV
    sq = h[..., o0:o0 + SQ]; o0 += SQ
    sk = h[..., o0:o0 + SK]; o0 += SK
    sv = h[..., o0:o0 + SV]

    dq = apply_rope(dq.reshape(B, S, 2 * DIFF_HEADS, HEAD_DIM), cos, sin)
    dk = apply_rope(dk.reshape(B, S, 2 * DIFF_HEADS, HEAD_DIM), cos, sin)
    dq = dq.reshape(B, S, DIFF_HEADS, 2, HEAD_DIM)
    dk = dk.reshape(B, S, DIFF_HEADS, 2, HEAD_DIM)
    dv = dv.reshape(B, S, DIFF_HEADS, 2 * HEAD_DIM)
    lv = lam_vec.astype(jnp.float32)
    lam = jnp.exp(jnp.sum(lv[0] * lv[1])) - jnp.exp(jnp.sum(lv[2] * lv[3])) + lambda_init
    y_diff = diff_attention(dq, dk, dv, lam, subln_g, lambda_init)

    sq = apply_rope(sq.reshape(B, S, SWA_Q_HEADS_2, HEAD_DIM), cos, sin)
    sk = apply_rope(sk.reshape(B, S, SWA_KV_HEADS, HEAD_DIM), cos, sin)
    sv = sv.reshape(B, S, SWA_KV_HEADS, HEAD_DIM)
    y_swa = swa_sink_attention(sq, sk, sv, sink, mask)

    return jnp.concatenate([y_diff, y_swa], axis=-1) @ w_out

def second_inputs(seed: int = 0) -> dict:
    key = jax.random.key(seed)
    ks = jax.random.split(key, 14)
    f32 = jnp.float32
    x = jax.random.normal(ks[0], (BATCH, SEQ, D_MODEL), f32)
    positions = jnp.broadcast_to(jnp.arange(SEQ, dtype=jnp.int32)[None, :], (BATCH, SEQ))
    col_scale = jnp.concatenate([
        jnp.ones((DQ + DK,), f32), jnp.full((DV,), BETA, f32),
        jnp.ones((SQ + SK,), f32), jnp.full((SV,), BETA, f32)])
    w_in = jax.random.normal(ks[1], (DEPTH_2, D_MODEL, IN_COLS), f32) * (D_MODEL ** -0.5) * col_scale
    w_out = jax.random.normal(ks[2], (DEPTH_2, MIX_WIDTH, D_MODEL), f32) * (MIX_WIDTH ** -0.5) * BETA
    diff_lambda = jax.random.normal(ks[3], (DEPTH_2, 4, HEAD_DIM), f32) * 0.1
    diff_subln_g = 1.0 + 0.02 * jax.random.normal(ks[4], (DEPTH_2, 2 * HEAD_DIM), f32)
    swa_sink = 0.5 * jax.random.normal(ks[5], (DEPTH_2, SWA_Q_HEADS_2), f32)
    ffn1_w_in = jax.random.normal(ks[6], (DEPTH_2, D_MODEL, 2 * D_FF_2), f32) * (D_MODEL ** -0.5)
    ffn1_w_out = jax.random.normal(ks[7], (DEPTH_2, D_FF_2, D_MODEL), f32) * (D_FF_2 ** -0.5) * BETA
    ffn2_w_in = jax.random.normal(ks[8], (DEPTH_2, D_MODEL, 2 * D_FF_2), f32) * (D_MODEL ** -0.5)
    ffn2_w_out = jax.random.normal(ks[9], (DEPTH_2, D_FF_2, D_MODEL), f32) * (D_FF_2 ** -0.5) * BETA
    ln_g = 1.0 + 0.02 * jax.random.normal(ks[10], (DEPTH_2, 3, D_MODEL), f32)
    ln_b = 0.02 * jax.random.normal(ks[11], (DEPTH_2, 3, D_MODEL), f32)
    return {"x": x, "positions": positions, "w_in": w_in, "w_out": w_out,
            "diff_lambda": diff_lambda, "diff_subln_g": diff_subln_g, "swa_sink": swa_sink,
            "ffn1_w_in": ffn1_w_in, "ffn1_w_out": ffn1_w_out,
            "ffn2_w_in": ffn2_w_in, "ffn2_w_out": ffn2_w_out,
            "ln_g": ln_g, "ln_b": ln_b}

def second_block(x, positions, w_in, w_out, diff_lambda, diff_subln_g, swa_sink,
              ffn1_w_in, ffn1_w_out, ffn2_w_in, ffn2_w_out, ln_g, ln_b):
    S = x.shape[1]
    cos, sin = rope_tables_2(positions)
    mask = band_mask(S)
    for l in range(DEPTH_2):
        lambda_init = 0.8 - 0.6 * math.exp(-0.3 * l)
        x = layer_norm(ALPHA * x + 0.5 * swiglu(x, ffn1_w_in[l], ffn1_w_out[l]), ln_g[l, 0], ln_b[l, 0])
        mix = hybrid_mixer(x, cos, sin, mask, w_in[l], w_out[l], diff_lambda[l],
                           diff_subln_g[l], swa_sink[l], lambda_init)
        x = layer_norm(ALPHA * x + mix, ln_g[l, 1], ln_b[l, 1])
        x = layer_norm(ALPHA * x + 0.5 * swiglu(x, ffn2_w_in[l], ffn2_w_out[l]), ln_g[l, 2], ln_b[l, 2])
    return x


def setup_inputs(seed=0):
    out = dict(first_inputs(seed))
    for name, value in second_inputs(seed + 1).items():
        if name != "x":
            out[name + "_2"] = value
    return out


def reference(
    x, positions, ln1_g, w_in, q_norm_a, k_norm_a, q_norm_b, k_norm_b, sinks, w_branch_a,
    w_branch_b, w_out, ln2_g, w_up, w_down, positions_2, w_in_2, w_out_2, diff_lambda_2,
    diff_subln_g_2, swa_sink_2, ffn1_w_in_2, ffn1_w_out_2, ffn2_w_in_2, ffn2_w_out_2, ln_g_2,
    ln_b_2,
):
    x = first_block(
        x, positions, ln1_g, w_in, q_norm_a, k_norm_a, q_norm_b, k_norm_b, sinks, w_branch_a,
        w_branch_b, w_out, ln2_g, w_up, w_down,
    )
    return second_block(
        x, positions_2, w_in_2, w_out_2, diff_lambda_2, diff_subln_g_2, swa_sink_2, ffn1_w_in_2,
        ffn1_w_out_2, ffn2_w_in_2, ffn2_w_out_2, ln_g_2, ln_b_2,
    )


_drawn_inputs = setup_inputs


def setup_inputs(seed=0):
    import zlib

    import numpy as np

    out = dict(_drawn_inputs(seed))
    spreads = {}
    factors = {'ln1_g': 8.0,
     'q_norm_a': 8.0,
     'k_norm_a': 8.0,
     'q_norm_b': 8.0,
     'k_norm_b': 8.0,
     'sinks': 64.0,
     'ln2_g': 9.488,
     'diff_lambda_2': 2.891,
     'diff_subln_g_2': 8.0,
     'swa_sink_2': 64.0}
    for name, (base, spread) in spreads.items():
        noise = np.random.default_rng([zlib.crc32(name.encode()), seed]).standard_normal(out[name].shape)
        drawn = base * np.exp(spread * noise) if base else spread * noise
        out[name] = __import__('jax').numpy.asarray(drawn.astype(out[name].dtype))
    for name, factor in factors.items():
        out[name] = (out[name] * factor).astype(out[name].dtype)
    return out
```

```python
import math
from contextlib import ExitStack

import numpy as np
import concourse.bass as bass
from concourse import mybir

P = 128
TOK = 256
TT = TOK // P
DM = 1024
KD = DM // P
HD = 64
N1 = 5120
DIL_W = 768
DIL_G, DIL_SLOTS = 3, 4
V1, QB1, KB1, VB1, QKV1 = 2 * DIL_W, 3 * DIL_W, 3 * DIL_W + 512, 3 * DIL_W + 640, 3 * DIL_W + 768
OA_W = DIL_SLOTS * HD
FF1 = 4 * DM
N2 = 2304
DK2, DV2, SQ2, SK2, SV2 = 512, 1024, 1536, 2048, 2176
FF2 = 2816
LAYERS = 2
KV = 2
ALPHA = (2.0 * LAYERS) ** 0.25
EPS1, EPS2 = 1e-6, 1e-5
LAMBDA_INIT = [0.8 - 0.6 * math.exp(-0.3 * l) for l in range(LAYERS)]
SCALE = HD ** -0.5
NEG = -1e30
ROPE1, ROPE2 = 8, 32
ROPES = ROPE1 + ROPE2
INV_FREQ = [float(v) for v in np.concatenate([
    np.float32(500000.0) ** (-np.arange(0, 16, 2, dtype=np.float32) / np.float32(16)),
    np.float32(10000.0) ** (-np.arange(0, 64, 2, dtype=np.float32) / np.float32(64))]).astype(np.float32)]
TWO_PI = (6.28125, 1.9350051879882812e-3, 3.0199159819567528e-7)
ROUND = 1.5 * 2.0 ** 23
PI_LOW = 3.1415925

SLOTS = 3
BW = 512
STRIP = (3, 3, 2)
S1 = N1 // BW
S1_GATES = QKV1 // BW
S1_SOLID = 7
STEP_BLOCKS = (1, 1, 1, 1, 1, 1, 1, 1, 1, 1, 2, 2, 2, 2, 2, 2, 2, 0)
NORMS = ((24, 0), (24, 0), (10, QB1), (10, QB1))
MLP_S = FF1 // BW
FFN_H = BW // 2
FFN_S = FF2 // FFN_H
PROJ2 = ((0, BW), (DK2, BW), (SQ2, BW), (SK2, 2 * KV * HD), (DV2, BW))
S2 = len(PROJ2)
T_BRANCH = S1
T_WOUT1 = T_BRANCH + 1
T_MLP = T_WOUT1 + 2
T_LAYER = T_MLP + 2 * MLP_S
L_PROJ = FFN_S
L_WOUT = L_PROJ + S2
L_FFN2 = L_WOUT + 2
L_TRIPLES = L_FFN2 + FFN_S
UNITS = 16
XT1 = 4
QK1_TILES, QK2_TILES = 17, 13
QK1_BANKS, QK2_BANKS = 9, 7

F32 = mybir.dt.float32
F32R = mybir.dt.float32r
BF16 = mybir.dt.bfloat16
I32 = mybir.dt.int32
ALU = mybir.AluOpType
ACT = mybir.ActivationFunctionType
AX = mybir.AxisListType


def build(nc, x, positions, ln1_g, w_in, q_norm_a, k_norm_a, q_norm_b, k_norm_b, sinks, w_branch_a,
          w_branch_b, w_out, ln2_g, w_up, w_down, positions_2, w_in_2, w_out_2, diff_lambda_2,
          diff_subln_g_2, swa_sink_2, ffn1_w_in_2, ffn1_w_out_2, ffn2_w_in_2, ffn2_w_out_2,
          ln_g_2, ln_b_2, out):
    ds = bass.ds
    w_in_r = w_in[0].rearrange("(k p) n -> p k n", p=P)
    wa_r = w_branch_a[0].rearrange("(k p) n -> p k n", p=P)
    wb_r = w_branch_b[0].rearrange("(k p) n -> p k n", p=P)
    w_out_r = w_out[0].rearrange("(k p) n -> p k n", p=P)
    w_up_r = w_up[0].rearrange("(k p) n -> p k n", p=P)
    w_down_r = w_down[0].rearrange("(s k p) n -> s p k n", p=P, k=BW // P)
    w_in2_r = w_in_2.rearrange("l (k p) n -> l p k n", p=P)
    w_out2_r = w_out_2.rearrange("l (k p) n -> l p k n", p=P)
    ffn_in_r = [w.rearrange("l (k p) n -> l p k n", p=P) for w in (ffn1_w_in_2, ffn2_w_in_2)]
    ffn_out_r = [w.rearrange("l (s k p) n -> l s p k n", p=P, k=FFN_H // P) for w in (ffn1_w_out_2, ffn2_w_out_2)]
    x_r = x[0].rearrange("(t p) n -> p t n", p=P)
    out_r = out[0].rearrange("(t p) n -> p t n", p=P)

    ctx = ExitStack()
    with ctx:
        def sb(name, shape, dt=F32):
            return ctx.enter_context(nc.sbuf_tensor(name, shape, dt))

        def sem(name):
            return ctx.enter_context(nc.semaphore(name))

        raw = [sb(f"raw{j}", [P, 4, BW]) for j in range(SLOTS)]
        whi = [sb(f"whi{j}", [P, 4, BW], F32R) for j in range(SLOTS)]
        wlo = [sb(f"wlo{j}", [P, 4, BW], F32R) for j in range(SLOTS)]
        xres = sb("xres", [P, TT, DM])
        xt_hi = sb("xt_hi", [P, KD, TOK], F32R)
        xt_lo = sb("xt_lo", [P, KD, TOK], F32R)
        ht_hi = sb("ht_hi", [P, BW // P, TOK], F32R)
        ht_lo = sb("ht_lo", [P, BW // P, TOK], F32R)
        proj = sb("proj", [P, TT, QKV1])
        gates = sb("gates", [P, TT, 2 * DM])
        qkt = sb("qkt", [P, QK1_TILES, TOK])
        ebuf = [sb(f"ebuf{j}", [P, 3 * TOK]) for j in range(3)]
        ptb = [sb(f"ptb{j}", [P, 3 * TOK]) for j in range(2)]
        square = sb("square", [P, 2 * DIL_W])
        ln_g = sb("ln_g", [P, DM])
        ln_b = sb("ln_b", [P, DM])
        mask = sb("mask", [P, 6, TOK], BF16)
        ident = sb("ident", [P, P])
        dist = sb("dist", [P, P], I32)
        dist4 = sb("dist4", [P, 2, P], I32)
        gain = sb("gain", [P, 4, HD])
        pos_i = sb("pos_i", [P, 2, TT], I32)
        pos_f = sb("pos_f", [P, 2, TT])
        inv = sb("inv", [P, ROPES])
        ang = sb("ang", [P, TT, ROPES])
        turns = sb("turns", [P, TT, ROPES])
        part = sb("part", [P, TT, ROPES])
        cosb = sb("cosb", [P, TT, ROPES])
        sinb = sb("sinb", [P, TT, ROPES])
        rope = sb("rope", [P, 4, 8 * ROPE2])
        half = sb("half", [P, 24])
        ln_eps = sb("ln_eps", [P, 1])
        per_head = sb("per_head", [P, 1])
        ssum = sb("ssum", [P, 24])
        rstd = sb("rstd", [P, 24])
        stats = sb("stats", [P, TT, 2, 6])
        mv = sb("mv", [P, TT, 2])
        lrs = sb("lrs", [P, TT])
        top = sb("top", [P, 4, 2])
        ntop = sb("ntop", [P, 4, 2])
        dsink = sb("dsink", [P, 4, 2])
        esink = sb("esink", [P, 4, 2])
        den = sb("den", [P, 4, 2])
        rden = sb("rden", [P, 4, 2])
        sink1 = sb("sink1", [P, 8])
        sink2 = sb("sink2", [P, LAYERS, 8])
        sinkc = sb("sinkc", [P, 8])
        dlam = sb("dlam", [P, LAYERS, 4, HD])
        dprod = sb("dprod", [P, LAYERS, 2, HD])
        dsum = sb("dsum", [P, LAYERS, 2])
        dexp = sb("dexp", [P, LAYERS, 2])
        lam = sb("lam", [P, LAYERS])
        second = sb("second", [P, 2 * HD])
        lamc = sb("lamc", [P, 1])
        subg = sb("subg", [P, LAYERS, 2 * HD])
        subgc = sb("subgc", [P, 2 * HD])
        dss = sb("dss", [P, TT * 4])
        drs = sb("drs", [P, TT * 4])
        normed = proj[:, :, 0:DM]
        hid_a = proj[:, :, 0:BW]
        hid_b = proj[:, :, BW:2 * BW]
        heads_out = proj[:, :, 0:DM]
        mixed = proj[:, :, DM:2 * DM]
        mix_b = proj[:, :, 2 * DM:3 * DM]
        ps = ctx.enter_context(nc.psum_tensor("ps", [P, 8, BW], F32))

        loaded = [sem(f"loaded{j}") for j in range(SLOTS)]
        hi_done = [sem(f"hi_done{j}") for j in range(SLOTS)]
        lo_done = [sem(f"lo_done{j}") for j in range(SLOTS)]
        used = [sem(f"used{j}") for j in range(SLOTS)]
        x_loaded = sem("x_loaded")
        const_loaded = sem("const_loaded")
        g_loaded = sem("g_loaded")
        ident_ready = sem("ident_ready")
        mask_pool = sem("mask_pool")
        mask_mod = sem("mask_mod")
        consts_set = sem("consts_set")
        ang_ready = sem("ang_ready")
        trig_ready = sem("trig_ready")
        lam_sum = sem("lam_sum")
        lam_exp = sem("lam_exp")
        rms_sum = sem("rms_sum")
        rms_rstd = sem("rms_rstd")
        xt_src = sem("xt_src")
        xt_tr = sem("xt_tr")
        xt_hi_done = sem("xt_hi_done")
        xt_lo_done = sem("xt_lo_done")
        proj_out = sem("proj_out")
        gate_half = sem("gate_half")
        head_sq = sem("head_sq")
        head_ss = sem("head_ss")
        head_rstd = sem("head_rstd")
        roped = sem("roped")
        qk_tr = sem("qk_tr")
        qk_out = sem("qk_out")
        s_ready = sem("s_ready")
        top_ready = sem("top_ready")
        e_ready = sem("e_ready")
        pt_ready = sem("pt_ready")
        pt_out = sem("pt_out")
        o_ready = sem("o_ready")
        o_out = sem("o_out")
        dsq = sem("dsq")
        dsum_ready = sem("dsum_ready")
        drs_ready = sem("drs_ready")
        hid_act = sem("hid_act")
        hid_ready = sem("hid_ready")
        hid_tr = sem("hid_tr")
        in_tile0 = sem("in_tile0")
        y_tile0 = sem("y_tile0")
        ht_hi_done = sem("ht_hi_done")
        ht_lo_done = sem("ht_lo_done")
        res_ready = sem("res_ready")
        var_ready = sem("var_ready")
        lrs_ready = sem("lrs_ready")
        stored = sem("stored")

        def mlp_up(s):
            return T_MLP if isinstance(s, int) and s == 0 else T_MLP + 2 * s - 1

        def dil_unit(u):
            return u // TT, u % TT

        def pair_unit(u):
            return (u - UNITS // 2) // TT, u % TT

        def masked_rows(first, u):
            if first and u < UNITS // 2:
                w = (u % TT + 1) * P
                return [[(g * w, w, g) for g in range(DIL_G)]]
            w = (u % TT + 1) * P if first else TOK
            kind = 3 if first else 4 + u % TT
            return [[(r * w, w, kind)] for r in range(KV)]

        def mask_of(kind, w):
            return mask[:, kind, TOK - w:TOK]

        def load(sp, slot, t, dst, src, inc=32):
            if not isinstance(t, int) or t > 0:
                sp.wait_ge(lo_done[slot], t)
            sp.dma_start(dst, src).then_inc(loaded[slot], inc)

        def load_strip(sp, t, w, col, width):
            k = 0
            for j, n in enumerate(STRIP):
                load(sp, j, t, raw[j][:, 0:n, 0:width], w[:, k:k + n, ds(col, width)])
                k += n

        def load_ffn_in(sp, t, w, l, s):
            for j in range(2):
                load(sp, j, t, raw[j][:, :, FFN_H:BW], w[l, :, 4 * j:4 * j + 4, ds(s * FFN_H + FF2, FFN_H)], 16)
                sp.dma_start(raw[j][:, :, 0:FFN_H], w[l, :, 4 * j:4 * j + 4, ds(s * FFN_H, FFN_H)]).then_inc(loaded[j], 16)

        def load_ffn_out(sp, t, w, l, s):
            load(sp, 2, t, raw[2][:, :, :].rearrange("p (k h) n -> p k (h n)", h=2), w[l, s, :, :, :])

        def load_down(sp, t, s):
            k = 0
            for j, n in enumerate((2, 1, 1)):
                load(sp, j, t, raw[j][:, 0:2 * n, :].rearrange("p (k h) n -> p k (h n)", h=2),
                     w_down_r[s, :, k:k + n, :])
                k += n

        def load_ln(sp, l, j):
            n = XT1 * (l + 1) + (0, 1, 3)[j]
            sp.wait_ge(xt_src, 2 * n + 2)
            sp.dma_start(ln_g[:, :], ln_g_2[l, j, :].partition_broadcast(P)).then_inc(g_loaded, 16)
            sp.dma_start(ln_b[:, :], ln_b_2[l, j, :].partition_broadcast(P)).then_inc(g_loaded, 16)

        def load_ffn(sp, t, f, l):
            wi, wo = ffn_in_r[f], ffn_out_r[f]
            load_ffn_in(sp, t + 1, wi, l, 1)
            load_ffn_out(sp, t, wo, l, 0)
            load_ffn_in(sp, t + 2, wi, l, 2)
            load_ffn_out(sp, t + 1, wo, l, 1)
            load_ln(sp, l, 2 * f)
            with sp.Fori(3, FFN_S) as s:
                load_ffn_in(sp, t + s, wi, l, s)
                load_ffn_out(sp, t + s - 1, wo, l, s - 1)

        def load_strip2(sp, t, l, j, slots):
            col, width = PROJ2[j]
            for q in slots:
                k = sum(STRIP[:q])
                load(sp, q, t, raw[q][:, 0:STRIP[q], 0:width], w_in2_r[l, :, k:k + STRIP[q], col:col + width])

        block = ctx.enter_context(nc.Block())

        @block.sync
        def _(sp):
            for t in range(TT):
                sp.dma_start(xres[:, t, :], x_r[:, t, :]).then_inc(x_loaded, 16)
            sp.dma_start(ln_g[:, :], ln1_g[0, :].partition_broadcast(P)).then_inc(g_loaded, 16)
            load_strip(sp, 0, w_in_r, 0, BW)
            with sp.Fori(1, S1) as s:
                load_strip(sp, s, w_in_r, s * BW, BW)
            load(sp, 0, T_BRANCH, raw[0][:, :, :].rearrange("p (k h) n -> p k (h n)", h=2), wa_r[:, 0:2, :])
            for j in (1, 2):
                load(sp, j, T_BRANCH, raw[j][:, :, :].rearrange("p (k h) n -> p k (h n)", h=2),
                     wb_r[:, 2 * j - 2:2 * j, :])
            for s in range(2):
                load_strip(sp, T_WOUT1 + s, w_out_r, s * BW, BW)
            sp.wait_ge(xt_src, 2)
            sp.dma_start(ln_g[:, :], ln2_g[0, :].partition_broadcast(P)).then_inc(g_loaded, 16)
            load_strip(sp, T_MLP, w_up_r, 0, BW)
            with sp.Fori(1, MLP_S) as s:
                load_strip(sp, T_MLP - 1 + s * 2, w_up_r, s * BW, BW)
                load_down(sp, T_MLP + s * 2, s - 1)
            load_down(sp, T_LAYER - 1, MLP_S - 1)
            load_ffn_in(sp, T_LAYER, ffn_in_r[0], 0, 0)
            with sp.Fori(0, LAYERS) as l:
                t = T_LAYER + L_TRIPLES * l
                load_ffn(sp, t, 0, l)
                load_strip2(sp, t + L_PROJ, l, 0, (0, 1))
                load_ffn_out(sp, t + FFN_S - 1, ffn_out_r[0], l, FFN_S - 1)
                load_strip2(sp, t + L_PROJ, l, 0, (2,))
                for j in range(1, S2):
                    load_strip2(sp, t + L_PROJ + j, l, j, (0, 1, 2))
                load_ln(sp, l, 1)
                for s in range(2):
                    load_strip(sp, t + L_WOUT + s, w_out2_r[l], s * BW, BW)
                load_ffn_in(sp, t + L_FFN2, ffn_in_r[1], l, 0)
                load_ffn(sp, t + L_FFN2, 1, l)
                load_ffn_in(sp, t + L_TRIPLES, ffn_in_r[0], LAYERS - 1, 0)
                load_ffn_out(sp, t + L_FFN2 + FFN_S - 1, ffn_out_r[1], l, FFN_S - 1)
            for t in range(TT):
                sp.wait_ge(xt_src, 2 * (XT1 + XT1 * LAYERS) + t + 1)
                sp.dma_start(out_r[:, t, :], xres[:, t, :]).then_inc(stored, 16)
            sp.wait_ge(stored, 16 * TT)


        def rsqrt(pool, dst, src, scale, eps, done):
            pool.tensor_scalar(dst, src, scale, eps, ALU.mult, ALU.add)
            pool.drain()
            pool.tensor_tensor(dst, dst, half[:, 0:dst.shape[-1]], ALU.pow).then_inc(done, 1)

        def norm_pool(pool, q, T, n):
            for t in range(TT):
                for b in ((0, 1), range(2, n))[t]:
                    if b == 0:
                        pool.wait_ge(hi_done[1], T + 1)
                    m = pool.tensor_tensor(wlo[1][:, b, :], raw[1][:, b, :], whi[1][:, b, :].bitcast(F32), ALU.subtract)
                if t == 1:
                    m.then_inc(lo_done[1], 1)
                pool.wait_ge(var_ready, 2 * q + t + 1)
                pool.tensor_tensor(lrs[:, t:t + 1], mv[:, t, 1:2], ln_eps[:, :], ALU.add)
                pool.drain()
                pool.tensor_tensor(lrs[:, t:t + 1], lrs[:, t:t + 1], half[:, 0:1], ALU.pow).then_inc(lrs_ready, 1)

        def rms_pool(pool, i):
            for t in range(TT):
                pool.wait_ge(rms_sum, 2 * i + t + 1)
                rsqrt(pool, lrs[:, t:t + 1], mv[:, t, 1:2], 1.0 / DM, EPS1, rms_rstd)

        @block.gpsimd
        def _(pool):
            pool.memset(half[:, :], -0.5)
            pool.memset(ln_eps[:, :], EPS2 / ALPHA ** 2)
            pool.memset(per_head[:, :], 1.0 / (2 * HD))
            pool.memset(ident[:, :], 0.0)
            pool.drain()
            pool.affine_select(out=ident[:, :], in_=ident[:, :], compare_op=ALU.not_equal, fill=1.0,
                               base=0, pattern=[[-1, P]], channel_multiplier=1).then_inc(ident_ready, 1)
            with nc.allow_non_contiguous_dma(reason="positions, one to a partition"):
                pool.dma_start(pos_i[:, 0, :], positions.rearrange("a (t p) -> p (a t)", p=P)).then_inc(const_loaded, 16)
                pool.dma_start(pos_i[:, 1, :], positions_2.rearrange("a (t p) -> p (a t)", p=P)).then_inc(const_loaded, 16)
            for j, g in enumerate((q_norm_a, k_norm_a, q_norm_b, k_norm_b)):
                pool.dma_start(gain[:, j, :], g[0, :].partition_broadcast(P)).then_inc(const_loaded, 16)
            pool.dma_start(sink1[:, :], sinks[0, :].partition_broadcast(P)).then_inc(const_loaded, 16)
            pool.dma_start(sink2[:, :, :], swa_sink_2.partition_broadcast(P)).then_inc(const_loaded, 16)
            pool.dma_start(subg[:, :, :], diff_subln_g_2.partition_broadcast(P)).then_inc(const_loaded, 16)
            pool.dma_start(dlam[:, :, :, :], diff_lambda_2.partition_broadcast(P)).then_inc(const_loaded, 16)
            rms_pool(pool, 0)
            for j, f in enumerate(INV_FREQ):
                pool.memset(inv[:, j:j + 1], f)
            pool.memset(mask[:, :, :], 0.0)
            pool.iota(dist[:, :], [[1, P]], base=P, channel_multiplier=-1).then_inc(consts_set, 1)
            pool.drain()
            pool.wait_ge(mask_mod, 1)
            for kind in range(5):
                pool.affine_select(out=mask[:, kind, P:TOK], in_=mask[:, kind, P:TOK], compare_op=ALU.is_ge,
                                   fill=NEG, base=0, pattern=[[-1, P]], channel_multiplier=1)
            for kind, least in ((0, 0), (5, 0), (3, 1)):
                pool.affine_select(out=mask[:, kind, 0:P], in_=mask[:, kind, 0:P], compare_op=ALU.is_ge,
                                   fill=NEG, base=-least, pattern=[[1, P]], channel_multiplier=-1)
            pool.drain().then_inc(mask_pool, 1)
            for i, (heads, _) in enumerate(NORMS):
                pool.wait_ge(head_ss, i + 1)
                rsqrt(pool, rstd[:, 0:heads], ssum[:, 0:heads], 1.0 / HD, EPS1, head_rstd)
            for s in range(S1_GATES, S1):
                pool.wait_ge(proj_out, 2 * s + 2)
                g = gates[:, :, (s - S1_GATES) * BW:(s - S1_GATES + 1) * BW]
                pool.tensor_scalar(g, g, 0.5, 0.5, ALU.mult, ALU.add).then_inc(gate_half, 1)
            rms_pool(pool, 1)
            with pool.Fori(0, LAYERS) as l:
                q = 3 * l
                norm_pool(pool, q, T_LAYER + L_TRIPLES * l + L_PROJ, STRIP[1])
                pool.wait_ge(o_out, UNITS * (l + 1) + UNITS // 2)
                pool.tensor_tensor(square[:, 0:TT * BW].rearrange("p (t n) -> p t n", t=TT), heads_out[:, :, 0:BW],
                                   heads_out[:, :, 0:BW], ALU.mult).then_inc(dsq, 1)
                pool.wait_ge(dsum_ready, l + 1)
                pool.tensor_tensor(drs[:, :], dss[:, :], per_head[:, :].to_broadcast([P, TT * 4]), ALU.mult)
                pool.drain()
                pool.tensor_scalar(drs[:, :], drs[:, :], 1.0, EPS2, ALU.mult, ALU.add)
                pool.drain()
                pool.tensor_tensor(drs[:, :], drs[:, :], half[:, 0:TT * 4], ALU.pow).then_inc(drs_ready, 1)
                norm_pool(pool, q + 1, T_LAYER + L_TRIPLES * l + L_FFN2, 4)
                norm_pool(pool, q + 2, T_LAYER + L_TRIPLES * (l + 1), 4)

        def split_hi(act, slot, t, n, width=BW):
            act.wait_ge(loaded[slot], 32 * (t + 1))
            if not isinstance(t, int) or t > 0:
                act.wait_ge(used[slot], t)
            act.activation(whi[slot][:, 0:n, 0:width], raw[slot][:, 0:n, 0:width], ACT.Copy).then_inc(hi_done[slot], 1)

        def split_lo(dve, slot, t, n, width=BW):
            dve.wait_ge(hi_done[slot], t + 1)
            dve.tensor_tensor(wlo[slot][:, 0:n, 0:width], raw[slot][:, 0:n, 0:width],
                              whi[slot][:, 0:n, 0:width].bitcast(F32), ALU.subtract).then_inc(lo_done[slot], 1)

        def split_round(split, eng, t, width=BW, after=(3, 3), after_width=BW):
            split(eng, 2, t, STRIP[2], width)
            split(eng, 0, t + 1, after[0], after_width)
            split(eng, 1, t + 1, after[1], after_width)

        def gate_plan():
            blocks, at = [], 0
            for n in STEP_BLOCKS:
                blocks.append(range(at, at + n))
                at += n
            assert at == (S1 - S1_SOLID) * KD
            step_of = {b: i for i, r in enumerate(blocks) for b in r}
            ends = [step_of[s * KD + sum(STRIP[:j + 1]) - 1] for s in range(S1 - S1_SOLID) for j in range(SLOTS)]
            splits = {0: [(2, S1_SOLID, STRIP[2])]}
            for c in range(3, len(ends) + 3):
                s, j = S1_SOLID + c // 3, c % 3
                splits.setdefault(ends[c - 3] + 1, []).append((j, s, STRIP[j] if s < S1 else 4))
            reads = {ends[3 * s + 2] + 1: S1_SOLID + s for s in range(S1 - S1_SOLID)}
            return blocks, splits, reads

        def xt_act(act, n, tiles=KD, toks=range(TT)):
            for t in toks:
                for b in range(2):
                    m = min(4, tiles - 4 * b)
                    act.wait_ge(xt_tr, 4 * n + 2 * t + b + 1)
                    act.activation(xt_hi[:, 4 * b:4 * b + m, t * P:(t + 1) * P],
                                   ps[:, 2 * t + b, 0:m * P].rearrange("p (k n) -> p k n", k=m),
                                   ACT.Copy).then_inc(xt_hi_done, 1)

        def paired(ap, heads):
            return ap.rearrange("p (g r d) -> p r g d", r=KV, d=HD)[:, heads // 4]

        def read_strip(act, done, parts, banks, func=ACT.Copy, scale=1.0):
            act.wait_ge(used[2], done)
            for t in range(TT):
                for col, width, dst in parts:
                    src, d = ps[:, banks[t], col:col + width], dst(t)
                    if len(d.shape) == 3:
                        src = src.rearrange("p (g d) -> p g d", d=HD)
                    m = act.activation(d, src, func, scale=scale)
                m.then_inc(proj_out, 1)

        def read_proj1(act, s):
            c = s * BW
            plain = lambda a, z: (a, z - a, lambda t: proj[:, t, c + a:c + z])
            heads = lambda a, h: (a, 4 * HD, lambda t: paired(proj[:, t, QB1:QB1 + 8 * HD], h))
            if c < QB1 < c + BW:
                parts = [plain(0, QB1 - c), heads(QB1 - c, 0)]
            elif c < KB1 < c + BW:
                parts = [heads(0, 4), plain(KB1 - c, BW)]
            else:
                parts = [plain(0, BW)]
            read_strip(act, s + 1, parts, (2 * (s % 2), 2 * (s % 2) + 1))

        def read_gate(act, s):
            c = (s - S1_GATES) * BW
            read_strip(act, s + 1, [(0, BW, lambda t: gates[:, t, c:c + BW])], (0, 1), ACT.Tanh, 0.5)

        def read_proj2(act, t, j):
            col, width = PROJ2[j]
            if col == SQ2:
                parts = [(4 * r * HD, 4 * HD, lambda i, r=r: paired(proj[:, i, col:col + width], 4 * r)) for r in range(KV)]
            else:
                parts = [(0, width, lambda i: proj[:, i, col:col + width])]
            read_strip(act, t + L_PROJ + j + 1, parts, (2 * (j % 2), 2 * (j % 2) + 1))

        def read_qk(act, base, events, bank0, tiles, banks):
            for e in events:
                m = min(2, tiles - 2 * e)
                act.wait_ge(qk_tr, base + e + 1)
                act.activation(qkt[:, 2 * e:2 * e + m, :],
                               ps[:, bank0 + e % banks, 0:m * TOK].rearrange("p (k n) -> p k n", k=m),
                               ACT.Copy).then_inc(qk_out, 1)

        def set_of(first, u):
            b = 2 + 2 * (u % 2) if first else 2 * (u % 3)
            return ps[:, b:b + 2, :].rearrange("p b n -> p (b n)")

        def width_of(first, u):
            if first and u < UNITS // 2:
                return DIL_G * P * (u % TT + 1)
            if first:
                return KV * P * (u % TT + 1)
            return 2 * TOK

        def exps(act, first, base, u):
            act.wait_ge(top_ready, base + u + 1)
            i = u % 4
            e = ebuf[u % 3]
            if u < UNITS // 2:
                if first:
                    w = width_of(first, u)
                    act.activation(e[:, 0:w], e[:, 0:w], ACT.Exp, bias=ntop[:, i, 0:1],
                                   accum_out=den[:, i, 0:1]).then_inc(e_ready, 1)
                    return
                for r in range(2):
                    o = act.activation(e[:, r * TOK:(r + 1) * TOK], set_of(first, u)[:, r * BW:r * BW + TOK],
                                       ACT.Exp, bias=ntop[:, i, r:r + 1], scale=SCALE, accum_out=den[:, i, r:r + 1])
                o.then_inc(e_ready, 1)
                return
            w = width_of(first, u) // KV
            for r in range(KV):
                act.activation(e[:, r * w:(r + 1) * w], e[:, r * w:(r + 1) * w], ACT.Exp,
                               bias=ntop[:, i, r:r + 1], accum_out=den[:, i, r:r + 1])
            act.activation(esink[:, i, :], dsink[:, i, :], ACT.Exp).then_inc(e_ready, 1)

        def read_pt(act, first, base, u):
            w = width_of(first, u)
            act.wait_ge(pt_ready, base + u + 1)
            if u >= 2:
                act.wait_ge(o_ready, base + u - 1)
            act.activation(ptb[u % 2][:, 0:w], set_of(first, u)[:, 0:w], ACT.Copy).then_inc(pt_out, 1)

        def head_square(act, i):
            heads, col = NORMS[i]
            if i > 0:
                act.wait_ge(head_ss, i)
            act.drain()
            act.activation(square[:, 0:heads * HD], proj[:, i % 2, col:col + heads * HD], ACT.Square).then_inc(head_sq, 1)

        def rms_act(act, i, toks=range(TT)):
            for t in toks:
                if i > 0:
                    act.wait_ge(res_ready, t + 1)
                act.activation(normed[:, t, :], xres[:, t, :], ACT.Square,
                               accum_out=mv[:, t, 1:2]).then_inc(rms_sum, 1)

        def hidden_act(act, g, done, par, ffn, tile0=None):
            w = FFN_H if ffn else BW
            for t in range(TT):
                if tile0 is not None and t == 0:
                    act.wait_ge(in_tile0, tile0)
                elif tile0 is not None or t == 0:
                    act.wait_ge(used[1 if ffn else 2], done)
                act.activation(hid_a[:, t, 0:w], ps[:, 2 * par + t, 0:w], ACT.Silu if ffn else ACT.Relu).then_inc(hid_act, 1)

        def ht_act(act, g, par, ffn):
            k = (FFN_H if ffn else BW) // P
            for t in range(TT):
                act.wait_ge(hid_tr, 2 * g + t + 1)
                act.activation(ht_hi[:, 0:k, t * P:(t + 1) * P], ps[:, 2 * par + t, 0:k * P].rearrange("p (k n) -> p k n", k=k),
                               ACT.Copy).then_inc(ht_hi_done, 1)

        def ffn_act(act, t, g, f, after):
            def step(s, par, n=(4, 4)):
                hidden_act(act, g + s - 1, t + s, 1 - par, True)
                split_hi(act, 2, t + s - 1, 4)
                ht_act(act, g + s - 1, 1 - par, True)
                split_hi(act, 0, t + s + 1, n[0])
                split_hi(act, 1, t + s + 1, n[1])
            split_hi(act, 0, t + 1, 4)
            split_hi(act, 1, t + 1, 4)
            step(1, 1)
            step(2, 0)
            with act.Fori(3, FFN_S - 2, 2) as s:
                step(s, 1)
                step(s + 1, 0)
            step(FFN_S - 2, 1)
            hidden_act(act, g + FFN_S - 2, t + FFN_S - 1, 1, True)
            split_hi(act, 2, t + FFN_S - 2, 4)
            ht_act(act, g + FFN_S - 2, 1, True)
            split_hi(act, 0, t + FFN_S, after[0])
            split_hi(act, 2, t + FFN_S - 1, 4)
            hidden_act(act, g + FFN_S - 1, t + FFN_S, 0, True, f + 1)
            ht_act(act, g + FFN_S - 1, 0, True)
            split_hi(act, 1, t + FFN_S, after[1])

        def mlp_split(split, eng, t, s, mid, after):
            split(eng, 2, t + 2 * s - 1, 2)
            mid()
            split(eng, 0, t + 2 * s, 4)
            split(eng, 1, t + 2 * s, 2)
            split(eng, 2, t + 2 * s, 2)
            split(eng, 0, t + 2 * s + 1, after[0])
            split(eng, 1, t + 2 * s + 1, after[1])

        @block.scalar
        def _(act):
            split_hi(act, 0, 0, 3)
            act.wait_ge(x_loaded, 16 * TT)
            rms_act(act, 0)
            split_hi(act, 1, 0, 3)
            xt_act(act, 0)
            for s in range(S1_SOLID):
                if s > 0:
                    read_proj1(act, s - 1)
                split_round(split_hi, act, s)
                if s == 2:
                    act.wait_ge(ang_ready, 1)
                    act.activation(sinb[:, :, :], ang[:, :, :], ACT.Sin)
                    act.activation(cosb[:, :, :], part[:, :, :], ACT.Sin).then_inc(trig_ready, 1)
                    act.wait_ge(lam_sum, 1)
                    act.activation(dexp[:, :, :], dsum[:, :, :], ACT.Exp).then_inc(lam_exp, 1)
                if s in (3, 4):
                    head_square(act, s - 3)
                if s == 6:
                    head_square(act, 2)
            head_square(act, 3)
            read_gate(act, S1_GATES)
            read_qk(act, 0, range(6), 6, QK1_TILES, 2)
            _, splits, reads = gate_plan()
            for i in range(UNITS + 2):
                if i == UNITS // 2:
                    read_qk(act, 0, range(6, QK1_BANKS), 6, QK1_TILES, 2)
                if i < UNITS:
                    exps(act, True, 0, i)
                if 1 <= i <= UNITS:
                    read_pt(act, True, 0, i - 1)
                if i in reads:
                    read_gate(act, reads[i])
                for j, s, n in splits.get(i, []):
                    split_hi(act, j, s, n)
            for i in sorted(k for k in (*splits, *reads) if k >= UNITS + 2):
                if i in reads:
                    read_gate(act, reads[i])
                for j, s, n in splits.get(i, []):
                    split_hi(act, j, s, n)
            xt_act(act, 1, 6)
            split_hi(act, 0, T_WOUT1, 3)
            split_hi(act, 1, T_WOUT1, 3)
            xt_act(act, 2)
            split_round(split_hi, act, T_WOUT1)
            split_hi(act, 2, T_WOUT1 + 1, STRIP[2])
            rms_act(act, 1, (0,))
            split_hi(act, 0, T_MLP, 3)
            split_hi(act, 1, T_MLP, 3)
            xt_act(act, 3, toks=(0,))
            rms_act(act, 1, (1,))
            xt_act(act, 3, toks=(1,))
            def step(s, par, after=(3, 3)):
                hidden_act(act, s - 1, mlp_up(s - 1) + 1, 1 - par, False)
                mlp_split(split_hi, act, T_MLP, s, lambda: ht_act(act, s - 1, 1 - par, False), after)
            split_round(split_hi, act, T_MLP)
            step(1, 1)
            with act.Fori(2, MLP_S - 2, 2) as s:
                step(s, 0)
                step(s + 1, 1)
            step(MLP_S - 2, 0)
            step(MLP_S - 1, 1, (4, 2))
            hidden_act(act, MLP_S - 1, mlp_up(MLP_S - 1) + 1, 1, False)
            ht_act(act, MLP_S - 1, 1, False)
            split_hi(act, 2, T_LAYER - 1, 2)
            split_hi(act, 0, T_LAYER, 4)
            split_hi(act, 1, T_LAYER, 4)
            with act.Fori(0, LAYERS) as l:
                t, g, n = T_LAYER + L_TRIPLES * l, MLP_S + 2 * FFN_S * l, XT1 * (l + 1)
                xt_act(act, n)
                ffn_act(act, t, g, 2 * l, STRIP)
                xt_act(act, n + 1)
                for j in range(S2):
                    if j > 0:
                        read_proj2(act, t, j - 1)
                    if j in (2, 3):
                        read_qk(act, QK1_BANKS + QK2_BANKS * l, (2 * j - 4, 2 * j - 3), 4, QK2_TILES, 3)
                    after = PROJ2[j + 1][1] if j + 1 < S2 else BW
                    split_round(split_hi, act, t + L_PROJ + j, PROJ2[j][1], after_width=after)
                read_qk(act, QK1_BANKS + QK2_BANKS * l, (4, 5, 6), 4, QK2_TILES, 3)
                read_proj2(act, t, S2 - 1)
                for i in range(UNITS + 2):
                    if i >= 2:
                        read_pt(act, False, UNITS * (l + 1), i - 2)
                    if i < UNITS:
                        exps(act, False, UNITS * (l + 1), i)
                    if i == 4:
                        split_hi(act, 2, t + L_WOUT, 2)
                xt_act(act, n + 2)
                split_hi(act, 0, t + L_WOUT + 1, 3)
                split_hi(act, 1, t + L_WOUT + 1, 3)
                split_round(split_hi, act, t + L_WOUT + 1, after=(4, 4))
                xt_act(act, n + 3)
                ffn_act(act, t + L_FFN2, g + FFN_S, 2 * l + 1, (4, 4))

        def xt_dve(dve, n, tiles=KD, toks=range(TT)):
            for t in toks:
                for b in range(2):
                    m = min(4, tiles - 4 * b)
                    ks, tok = slice(4 * b, 4 * b + m), slice(t * P, (t + 1) * P)
                    dve.wait_ge(xt_hi_done, 4 * n + 2 * t + b + 1)
                    dve.tensor_tensor(xt_lo[:, ks, tok], ps[:, 2 * t + b, 0:m * P].rearrange("p (k n) -> p k n", k=m),
                                      xt_hi[:, ks, tok].bitcast(F32), ALU.subtract).then_inc(xt_lo_done, 1)

        def maxima(dve, first, base, u):
            if u >= 3:
                dve.wait_ge(pt_ready, base + u - 2)
            dve.wait_ge(s_ready, base + u + 1)
            i = u % 4
            e, s = ebuf[u % 3], set_of(first, u)
            g = (u - UNITS // 2) // TT
            if u >= UNITS // 2:
                dve.tensor_copy(dsink[:, i, :], (sink1 if first else sinkc)[:, g:8:4])
            if u < UNITS // 2:
                if first:
                    w = width_of(first, u)
                    n = w // DIL_G
                    dve.tensor_tensor_reduce(e[:, 0:w].rearrange("p (g n) -> p g n", g=DIL_G),
                                             s[:, 0:w].rearrange("p (g n) -> p g n", g=DIL_G),
                                             mask[:, 0:DIL_G, TOK - n:TOK], SCALE, -3e38, ALU.add, ALU.max, top[:, i, 0:1])
                    dve.drain()
                    dve.tensor_scalar(ntop[:, i, 0:1], top[:, i, 0:1], -1.0, None, ALU.mult).then_inc(top_ready, 1)
                    return
                dve.tensor_reduce(top[:, i, :], s.rearrange("p (r n) -> p r n", r=2)[:, :, 0:TOK], AX.X, ALU.max)
                dve.drain()
                dve.tensor_scalar(ntop[:, i, :], top[:, i, :], -SCALE, None, ALU.mult).then_inc(top_ready, 1)
                return
            w = width_of(first, u) // KV
            kind = 3 if first else 4 + u % TT
            for r in range(KV):
                dve.tensor_tensor_reduce(e[:, r * w:(r + 1) * w], s[:, r * BW:r * BW + w], mask[:, kind, TOK - w:TOK],
                                         SCALE, -3e38, ALU.add, ALU.max, top[:, i, r:r + 1])
            dve.drain()
            dve.tensor_tensor(top[:, i, :], top[:, i, :], dsink[:, i, :], ALU.max)
            dve.drain()
            dve.tensor_tensor(dsink[:, i, :], dsink[:, i, :], top[:, i, :], ALU.subtract)
            dve.tensor_scalar(ntop[:, i, :], top[:, i, :], -1.0, None, ALU.mult).then_inc(top_ready, 1)

        def reciprocals(dve, first, base, u):
            dve.wait_ge(e_ready, base + u + 1)
            i = u % 4
            if first and u < UNITS // 2:
                dve.reciprocal(rden[:, i, 0:1], den[:, i, 0:1])
                return
            if u >= UNITS // 2:
                dve.tensor_tensor(den[:, i, :], den[:, i, :], esink[:, i, :], ALU.add)
                dve.drain()
                dve.reciprocal(rden[:, i, :], den[:, i, :])
                return
            dve.reciprocal(rden[:, i, :], den[:, i, :])
            dve.drain()
            dve.tensor_tensor(rden[:, i, 1:2], rden[:, i, 1:2], lamc[:, :], ALU.mult)

        def read_out(dve, first, base, u):
            dve.wait_ge(o_ready, base + u + 1)
            o, qt = ps[:, 6 + u % 2, :], u % TT
            if not first and u < UNITS // 2:
                h = u // TT
                dve.tensor_scalar(second[:, :], o[:, 2 * HD:4 * HD], rden[:, u % 4, 1:2], None, ALU.mult)
                dve.drain()
                dve.scalar_tensor_tensor(heads_out[:, qt, h * 2 * HD:(h + 1) * 2 * HD], o[:, 0:2 * HD],
                                         rden[:, u % 4, 0:1], second[:, :], ALU.mult, ALU.subtract).then_inc(o_out, 1)
                return
            if u < UNITS // 2:
                cols = [u // TT * HD]
            else:
                g = (u - UNITS // 2) // TT
                cols = [(OA_W if first else BW) + (4 * r + g) * HD for r in range(KV)]
            for r, c in enumerate(cols):
                m = dve.tensor_scalar(heads_out[:, qt, c:c + HD], o[:, r * HD:(r + 1) * HD],
                                      rden[:, u % 4, r:r + 1], None, ALU.mult)
            m.then_inc(o_out, 1)

        def sum_squares(dve, i):
            heads = NORMS[i][0]
            dve.wait_ge(head_sq, i + 1)
            dve.tensor_reduce(ssum[:, 0:heads], square[:, 0:heads * HD].rearrange("p (h d) -> p h d", d=HD),
                              AX.X, ALU.add).then_inc(head_ss, 1)

        def rotate(dve, x1, x2, cos, sin, t1, t2, t3, t4):
            dve.tensor_tensor(t1, x1, cos, ALU.mult)
            dve.tensor_tensor(t2, x2, sin, ALU.mult)
            dve.tensor_tensor(t3, x2, cos, ALU.mult)
            dve.tensor_tensor(t4, x1, sin, ALU.mult)
            dve.drain()
            dve.tensor_tensor(x1, t1, t2, ALU.subtract)
            return dve.tensor_tensor(x2, t3, t4, ALU.add)

        def norm_heads(dve, i):
            heads, col = NORMS[i]
            t = i % 2
            v = proj[:, t, col:col + heads * HD].rearrange("p (h d) -> p h d", d=HD)
            dve.wait_ge(head_rstd, i + 1)
            dve.tensor_tensor(v, v, rstd[:, 0:heads].unsqueeze(2).to_broadcast([P, heads, HD]), ALU.mult)
            dve.drain()
            if i < 2:
                g = v.rearrange("p (g h) d -> p g h d", g=2)
                dve.tensor_tensor(g, g, gain[:, 0:2, :].unsqueeze(2).to_broadcast([P, 2, 12, HD]), ALU.mult)
            else:
                dve.tensor_tensor(v[:, 0:8, :], v[:, 0:8, :], gain[:, 2:3, :].to_broadcast([P, 8, HD]), ALU.mult)
                dve.tensor_tensor(v[:, 8:10, :], v[:, 8:10, :], gain[:, 3:4, :].to_broadcast([P, 2, HD]), ALU.mult)
            dve.drain()
            if i == 0:
                dve.wait_ge(trig_ready, 1)
            tmp = [rope[:, j, 0:heads * ROPE1].rearrange("p (h d) -> p h d", d=ROPE1) for j in range(4)]
            c, s = (z[:, t:t + 1, 0:ROPE1].to_broadcast([P, heads, ROPE1]) for z in (cosb, sinb))
            rotate(dve, v[:, :, 0:ROPE1], v[:, :, ROPE1:2 * ROPE1], c, s, *tmp).then_inc(roped, 1)

        def rotate_strip(dve, l, j):
            col = PROJ2[j][0]
            heads = 2 if col == SK2 else 8
            dve.drain()
            dve.wait_ge(proj_out, 2 * (S1 + S2 * l + j) + 2)
            for t in range(TT):
                v = proj[:, t, col:col + heads * HD].rearrange("p (h r d) -> p h r d", r=2, d=ROPE2)
                tmp = [rope[:, i, 0:heads * ROPE2].rearrange("p (h d) -> p h d", d=ROPE2) for i in range(4)]
                c, s = (z[:, t:t + 1, ROPE1:ROPES].to_broadcast([P, heads, ROPE2]) for z in (cosb, sinb))
                if t > 0:
                    dve.drain()
                m = rotate(dve, v[:, :, 0, :], v[:, :, 1, :], c, s, *tmp)
            m.then_inc(roped, 1)

        def rms_dve(dve, i, toks=range(TT)):
            dve.wait_ge(g_loaded, 16 * (i + 1))
            for t in toks:
                dve.wait_ge(rms_rstd, 2 * i + t + 1)
                dve.scalar_tensor_tensor(normed[:, t, :], xres[:, t, :], lrs[:, t:t + 1], ln_g[:, :],
                                         ALU.mult, ALU.mult).then_inc(xt_src, 1)

        def hidden_dve(dve, g, par, ffn):
            w = FFN_H if ffn else BW
            for t in range(TT):
                dve.wait_ge(hid_act, 2 * g + t + 1)
                other = ps[:, 2 * par + t, w:2 * w] if ffn else hid_a[:, t, 0:w]
                dve.tensor_tensor(hid_b[:, t, 0:w], hid_a[:, t, 0:w], other, ALU.mult).then_inc(hid_ready, 1)

        def ht_dve(dve, g, par, ffn):
            k = (FFN_H if ffn else BW) // P
            for t in range(TT):
                tok = slice(t * P, (t + 1) * P)
                dve.wait_ge(ht_hi_done, 2 * g + t + 1)
                dve.tensor_tensor(ht_lo[:, 0:k, tok], ps[:, 2 * par + t, 0:k * P].rearrange("p (k n) -> p k n", k=k),
                                  ht_hi[:, 0:k, tok].bitcast(F32), ALU.subtract).then_inc(ht_lo_done, 1)

        def ffn_dve(dve, t, g, after0):
            def step(s, par, n=(4, 4)):
                hidden_dve(dve, g + s - 1, 1 - par, True)
                split_lo(dve, 2, t + s - 1, 4)
                ht_dve(dve, g + s - 1, 1 - par, True)
                split_lo(dve, 0, t + s + 1, n[0])
                split_lo(dve, 1, t + s + 1, n[1])
            split_lo(dve, 0, t + 1, 4)
            split_lo(dve, 1, t + 1, 4)
            step(1, 1)
            step(2, 0)
            with dve.Fori(3, FFN_S - 2, 2) as s:
                step(s, 1)
                step(s + 1, 0)
            step(FFN_S - 2, 1)
            hidden_dve(dve, g + FFN_S - 2, 1, True)
            split_lo(dve, 2, t + FFN_S - 2, 4)
            ht_dve(dve, g + FFN_S - 2, 1, True)
            split_lo(dve, 0, t + FFN_S, after0)
            split_lo(dve, 2, t + FFN_S - 1, 4)
            hidden_dve(dve, g + FFN_S - 1, 0, True)
            ht_dve(dve, g + FFN_S - 1, 0, True)

        def norm_dve(dve, q, n, done, ffn, split=None):
            def add(t):
                if t == 0:
                    dve.wait_ge(y_tile0, q + 3)
                else:
                    dve.wait_ge(used[2], done)
                if ffn:
                    dve.scalar_tensor_tensor(xres[:, t, :], ps[:, 4 + 2 * t:6 + 2 * t, :].rearrange("p b n -> p (b n)"),
                                             0.5 / ALPHA, xres[:, t, :], ALU.mult, ALU.add)
                else:
                    dve.scalar_tensor_tensor(xres[:, t, BW:DM], ps[:, 2 + t, :], 1.0 / ALPHA, xres[:, t, BW:DM],
                                             ALU.mult, ALU.add)

            def centre(t):
                dve.drain()
                for h in range(2):
                    dve.bn_stats(stats[:, t, h, :], xres[:, t, h * BW:(h + 1) * BW])
                dve.drain()
                dve.bn_aggr(mv[:, t, :], stats[:, t, :, :].rearrange("p h n -> p (h n)")).then_inc(var_ready, 1)
                dve.drain()
                if t == 0:
                    dve.wait_ge(g_loaded, 32 * (q + 2))
                dve.scalar_tensor_tensor(xres[:, t, :], xres[:, t, :], mv[:, t, 0:1], ln_g[:, :], ALU.subtract, ALU.mult)

            def scale(t):
                dve.drain()
                dve.wait_ge(lrs_ready, 2 * q + t + 1)
                dve.scalar_tensor_tensor(xres[:, t, :], xres[:, t, :], lrs[:, t:t + 1], ln_b[:, :],
                                         ALU.mult, ALU.add).then_inc(xt_src, 1)
            add(0)
            centre(0)
            scale(0)
            add(1)
            if split is not None:
                split()
            if n is not None:
                xt_dve(dve, n, toks=(0,))
            centre(1)
            scale(1)
            if n is not None:
                xt_dve(dve, n, toks=(1,))

        def angles(dve):
            dve.wait_ge(consts_set, 1)
            dve.wait_ge(const_loaded, 16 * 10)
            dve.tensor_copy(pos_f[:, :, :], pos_i[:, :, :])
            dve.drain()
            for t in range(TT):
                for b, (a, z) in enumerate(((0, ROPE1), (ROPE1, ROPES))):
                    dve.tensor_scalar(ang[:, t, a:z], inv[:, a:z], pos_f[:, b, t:t + 1], None, ALU.mult)
            dve.drain()
            dve.tensor_scalar(turns[:, :, :], ang[:, :, :], 1.0 / (2 * math.pi), ROUND, ALU.mult, ALU.add)
            dve.drain()
            dve.tensor_scalar(turns[:, :, :], turns[:, :, :], ROUND, None, ALU.subtract)
            for c in TWO_PI:
                dve.drain()
                dve.scalar_tensor_tensor(ang[:, :, :], turns[:, :, :], -c, ang[:, :, :], ALU.mult, ALU.add)
            dve.drain()
            dve.tensor_scalar(ang[:, :, :], ang[:, :, :], PI_LOW, -PI_LOW, ALU.min, ALU.max)
            dve.drain()
            dve.scalar_tensor_tensor(part[:, :, :], ang[:, :, :], -1.0, ang[:, :, :], ALU.mult, ALU.min)
            dve.drain()
            dve.tensor_scalar(part[:, :, :], part[:, :, :], math.pi / 2, None, ALU.add).then_inc(ang_ready, 1)

        def stride_masks(dve):
            for b, bits in enumerate((3, 15)):
                dve.tensor_scalar(dist4[:, b, :], dist[:, :], bits, None, ALU.bitwise_and)
            dve.drain()
            for b in range(2):
                for j in range(2):
                    m = dve.tensor_scalar(mask[:, 1 + b, j * P:(j + 1) * P], dist4[:, b, :], 0.0, NEG,
                                          ALU.not_equal, ALU.mult)
            m.then_inc(mask_mod, 1)

        def lambdas_sums(dve):
            dve.tensor_tensor(dprod[:, :, :, :], dlam[:, :, 0:4:2, :], dlam[:, :, 1:4:2, :], ALU.mult)
            dve.drain()
            dve.tensor_reduce(dsum[:, :, :], dprod[:, :, :, :], AX.X, ALU.add).then_inc(lam_sum, 1)

        def lambdas(dve):
            dve.wait_ge(lam_exp, 1)
            for l, init in enumerate(LAMBDA_INIT):
                dve.scalar_tensor_tensor(lam[:, l:l + 1], dexp[:, l, 0:1], init, dexp[:, l, 1:2], ALU.add, ALU.subtract)
                dve.tensor_scalar(subg[:, l, :], subg[:, l, :], 1.0 - init, None, ALU.mult)

        @block.vector
        def _(dve):
            split_lo(dve, 0, 0, 3)
            rms_dve(dve, 0)
            split_lo(dve, 1, 0, 3)
            xt_dve(dve, 0)
            for s in range(S1_SOLID):
                split_round(split_lo, dve, s)
                if s == 0:
                    angles(dve)
                    stride_masks(dve)
                    lambdas_sums(dve)
                if s == 3:
                    lambdas(dve)
                    sum_squares(dve, 0)
                if s == 4:
                    norm_heads(dve, 0)
                    sum_squares(dve, 1)
                if s == 5:
                    norm_heads(dve, 1)
            sum_squares(dve, 2)
            norm_heads(dve, 2)
            sum_squares(dve, 3)
            _, splits, _ = gate_plan()
            dve.wait_ge(mask_pool, 1)
            for i in range(UNITS + 2):
                if i < UNITS:
                    maxima(dve, True, 0, i)
                if 1 <= i <= UNITS:
                    reciprocals(dve, True, 0, i - 1)
                if i >= 2:
                    if i == UNITS + 1:
                        dve.drain()
                    read_out(dve, True, 0, i - 2)
                if i == 2:
                    norm_heads(dve, 3)
                for j, s, n in splits.get(i, []):
                    split_lo(dve, j, s, n)
            dve.drain().then_inc(xt_src, 2)
            for i in sorted(k for k in splits if k >= UNITS + 2):
                for j, s, n in splits[i]:
                    split_lo(dve, j, s, n)
            xt_dve(dve, 1, 6)
            dve.wait_ge(gate_half, S1 - S1_GATES)
            dve.wait_ge(used[0], T_BRANCH + 1)
            for t in range(TT):
                dve.tensor_tensor(mixed[:, t, :], ps[:, 2 * t:2 * t + 2, :].rearrange("p b n -> p (b n)"),
                                  gates[:, t, 0:DM], ALU.mult)
            split_lo(dve, 0, T_WOUT1, 3)
            dve.wait_ge(used[2], T_BRANCH + 1)
            for t in range(TT):
                dve.tensor_tensor(mix_b[:, t, :], ps[:, 4 + 2 * t:6 + 2 * t, :].rearrange("p b n -> p (b n)"),
                                  gates[:, t, DM:2 * DM], ALU.mult)
                dve.drain()
                dve.tensor_tensor(mixed[:, t, :], mixed[:, t, :], mix_b[:, t, :], ALU.add).then_inc(xt_src, 1)
            split_lo(dve, 1, T_WOUT1, 3)
            xt_dve(dve, 2)
            split_round(split_lo, dve, T_WOUT1)
            dve.wait_ge(used[2], T_WOUT1 + 1)
            for t in range(TT):
                dve.tensor_tensor(xres[:, t, 0:BW], xres[:, t, 0:BW], ps[:, t, :], ALU.add)
            split_lo(dve, 2, T_WOUT1 + 1, STRIP[2])
            dve.wait_ge(y_tile0, 1)
            dve.tensor_tensor(xres[:, 0, BW:DM], xres[:, 0, BW:DM], ps[:, 2, :], ALU.add).then_inc(res_ready, 1)
            rms_dve(dve, 1, (0,))
            split_lo(dve, 0, T_MLP, 3)
            dve.wait_ge(used[2], T_WOUT1 + 2)
            dve.tensor_tensor(xres[:, 1, BW:DM], xres[:, 1, BW:DM], ps[:, 3, :], ALU.add).then_inc(res_ready, 1)
            xt_dve(dve, 3, toks=(0,))
            split_lo(dve, 1, T_MLP, 3)
            rms_dve(dve, 1, (1,))
            xt_dve(dve, 3, toks=(1,))
            def step(s, par, after=(3, 3)):
                hidden_dve(dve, s - 1, 1 - par, False)
                mlp_split(split_lo, dve, T_MLP, s, lambda: ht_dve(dve, s - 1, 1 - par, False), after)
            split_round(split_lo, dve, T_MLP)
            step(1, 1)
            with dve.Fori(2, MLP_S - 2, 2) as s:
                step(s, 0)
                step(s + 1, 1)
            step(MLP_S - 2, 0)
            step(MLP_S - 1, 1, (4, 2))
            hidden_dve(dve, MLP_S - 1, 1, False)
            ht_dve(dve, MLP_S - 1, 1, False)
            split_lo(dve, 2, T_LAYER - 1, 2)
            for t in range(TT):
                if t == 0:
                    dve.wait_ge(y_tile0, 2)
                else:
                    split_lo(dve, 0, T_LAYER, 4)
                    dve.wait_ge(used[2], T_LAYER)
                dve.tensor_tensor(xres[:, t, :], xres[:, t, :], ps[:, 4 + 2 * t:6 + 2 * t, :].rearrange("p b n -> p (b n)"),
                                  ALU.add).then_inc(xt_src, 1)
            split_lo(dve, 1, T_LAYER, 4)
            with dve.Fori(0, LAYERS) as l:
                t, g, n, q = T_LAYER + L_TRIPLES * l, MLP_S + 2 * FFN_S * l, XT1 * (l + 1), 3 * l
                base = UNITS * (l + 1)
                dve.drain()
                dve.tensor_copy(lamc[:, :], lam[:, ds(l, 1)])
                dve.tensor_copy(sinkc[:, :], sink2[:, ds(l, 1), :])
                dve.tensor_copy(subgc[:, :], subg[:, ds(l, 1), :])
                xt_dve(dve, n)
                ffn_dve(dve, t, g, STRIP[0])
                norm_dve(dve, q, n + 1, t + FFN_S, True)
                for j in range(S2):
                    if j > 0:
                        rotate_strip(dve, l, j - 1)
                    after = PROJ2[j + 1][1] if j + 1 < S2 else BW
                    split_round(split_lo, dve, t + L_PROJ + j, PROJ2[j][1], after_width=after)
                for i in range(UNITS + 2):
                    if i < UNITS:
                        maxima(dve, False, base, i)
                    if 1 <= i <= UNITS:
                        reciprocals(dve, False, base, i - 1)
                    if i >= 2:
                        if i == UNITS + 1:
                            dve.drain()
                        read_out(dve, False, base, i - 2)
                    if i == 4:
                        split_lo(dve, 2, t + L_WOUT, 2)
                    if i == UNITS // 2 + 3:
                        dve.wait_ge(dsq, l + 1)
                        dve.tensor_reduce(dss[:, :].rearrange("p (t h) -> p t h", t=TT),
                                          square[:, 0:TT * BW].rearrange("p (t h d) -> p t h d", t=TT, d=2 * HD),
                                          AX.X, ALU.add).then_inc(dsum_ready, 1)
                    if i == UNITS // 2 + 5:
                        dve.wait_ge(drs_ready, l + 1)
                        v = heads_out[:, :, 0:BW].rearrange("p t (h d) -> p t h d", d=2 * HD)
                        for k in range(TT):
                            dve.tensor_tensor(v[:, k], v[:, k], drs[:, 4 * k:4 * k + 4].unsqueeze(2)
                                              .to_broadcast([P, 4, 2 * HD]), ALU.mult)
                        dve.drain()
                        for k in range(TT):
                            dve.tensor_tensor(v[:, k], v[:, k], subgc[:, :].unsqueeze(1)
                                              .to_broadcast([P, 4, 2 * HD]), ALU.mult)
                dve.drain().then_inc(xt_src, 2)
                xt_dve(dve, n + 2)
                split_lo(dve, 0, t + L_WOUT + 1, 3)
                split_lo(dve, 1, t + L_WOUT + 1, 3)
                dve.wait_ge(used[2], t + L_WOUT + 1)
                for k in range(TT):
                    xs = xres[:, k, 0:BW]
                    dve.scalar_tensor_tensor(xs, ps[:, k, :], 1.0 / ALPHA, xs, ALU.mult, ALU.add)
                split_lo(dve, 2, t + L_WOUT + 1, STRIP[2])
                norm_dve(dve, q + 1, n + 3, t + L_WOUT + 2, False, lambda: split_lo(dve, 0, t + L_FFN2, 4))
                ffn_dve(dve, t + L_FFN2, g + FFN_S, 4)
                norm_dve(dve, q + 2, None, t + L_TRIPLES, True)

        def block_mm(pe, hi, lo, k, slot, b, banks, start, stop, width=BW):
            for t in range(TT):
                o, tok = ps[:, banks[t], 0:width], slice(t * P, (t + 1) * P)
                pe.matmul(o, hi[:, k, tok], whi[slot][:, b, 0:width], start=start, stop=False)
                pe.matmul(o, hi[:, k, tok], wlo[slot][:, b, 0:width], start=False, stop=False)
                m = pe.matmul(o, lo[:, k, tok], whi[slot][:, b, 0:width], start=False, stop=stop)
            return m

        def tile_mm(pe, hi, lo, k, slot, b, t, bank, start, stop, width=BW):
            o, tok = ps[:, bank, 0:width], slice(t * P, (t + 1) * P)
            pe.matmul(o, hi[:, k, tok], whi[slot][:, b, 0:width], start=start, stop=False)
            pe.matmul(o, hi[:, k, tok], wlo[slot][:, b, 0:width], start=False, stop=False)
            return pe.matmul(o, lo[:, k, tok], whi[slot][:, b, 0:width], start=False, stop=stop)

        def strip_block(pe, t, k, banks, width=BW):
            slot = 0 if k < 3 else 1 if k < 6 else 2
            b = k - sum(STRIP[:slot])
            if b == 0:
                pe.wait_ge(lo_done[slot], t + 1)
            m = block_mm(pe, xt_hi, xt_lo, k, slot, b, banks, k == 0, k == KD - 1, width)
            if b == STRIP[slot] - 1:
                m.then_inc(used[slot], 1)

        def strip(pe, t, banks, width=BW, between=None, at=2):
            for k in range(KD):
                strip_block(pe, t, k, banks, width)
                if between is not None and k == at:
                    between()

        def pair(par):
            return (2 * par, 2 * par + 1)

        def xt_tile_pe(pe, n, t, src, tiles=KD):
            pe.wait_ge(xt_src, 2 * n + t + 1)
            for b in range(2):
                for i, k in enumerate(range(4 * b, min(4 * b + 4, tiles))):
                    m = pe.transpose(ps[:, 2 * t + b, i * P:(i + 1) * P], src[:, t, k * P:(k + 1) * P], ident[:, :])
                m.then_inc(xt_tr, 1)

        def first_strip(pe, n, src, T, chunks, width=BW, at=5):
            seq = [(slot, b) for slot, blocks in enumerate(chunks) for b in range(blocks)]
            xt_tile_pe(pe, n, 0, src)
            pe.wait_ge(xt_lo_done, 4 * n + 2)
            for t in range(TT):
                for k, (slot, b) in enumerate(seq):
                    if t == 0 and b == 0:
                        pe.wait_ge(lo_done[slot], T + 1)
                    m = tile_mm(pe, xt_hi, xt_lo, k, slot, b, t, t, k == 0, k == KD - 1, width)
                    if t == 1 and b == chunks[slot] - 1:
                        m.then_inc(used[slot], 1)
                    if t == 0 and k == at:
                        xt_tile_pe(pe, n, 1, src)
                if t == 0:
                    pe.wait_ge(xt_lo_done, 4 * n + 4)

        def last_strip(pe, T, bank0):
            for t in range(TT):
                for k in range(KD):
                    slot = 0 if k < 3 else 1 if k < 6 else 2
                    b = k - sum(STRIP[:slot])
                    if t == 0 and b == 0:
                        pe.wait_ge(lo_done[slot], T + 1)
                    m = tile_mm(pe, xt_hi, xt_lo, k, slot, b, t, bank0 + t, k == 0, k == KD - 1)
                    if t == 1 and b == STRIP[slot] - 1:
                        m.then_inc(used[slot], 1)
                if t == 0:
                    m.then_inc(y_tile0, 1)

        def xt_pe(pe, n, src, tiles=KD):
            for t in range(TT):
                xt_tile_pe(pe, n, t, src, tiles)
            pe.wait_ge(xt_lo_done, 4 * n + 4)

        def qk_pe(pe, base, events, bank0, banks, src, tiles):
            for e in events:
                if e >= banks:
                    pe.wait_ge(qk_out, base + e - banks + 1)
                for i in range(min(2, tiles - 2 * e)):
                    for t in range(TT):
                        m = pe.transpose(ps[:, bank0 + e % banks, (2 * i + t) * P:(2 * i + t + 1) * P],
                                         src(2 * e + i, t), ident[:, :])
                m.then_inc(qk_tr, 1)

        def qk_src1(tile, t):
            c = tile * P if tile < 12 else QB1 + (tile - 12) * P
            return proj[:, t, c:c + P]

        def qk_src2(tile, t):
            c = tile * P if tile < 8 else SQ2 + (tile - 8) * P
            return proj[:, t, c:c + P]

        def scores(pe, first, base, u):
            ns = 2 if first else 3
            if u >= ns:
                pe.wait_ge(pt_out, base + u - ns + 1)
            s, qt = set_of(first, u), u % TT
            n = P * (qt + 1) if first else TOK
            if u < UNITS // 2:
                h = u // TT
                if first:
                    parts = [(h % 2, 2 * g + h // 2, 6 + 2 * g + h // 2) for g in range(DIL_G)]
                else:
                    parts = [(c, h, 4 + h) for c in range(2)]
            else:
                g = (u - UNITS // 2) // TT
                parts = [(r, (12 if first else 8) + g, 16 if first else 12) for r in range(KV)]
            for i, (r, qtile, ktile) in enumerate(parts):
                rows = slice(r * HD, (r + 1) * HD)
                c = i * (n if len(parts) == DIL_G else BW)
                m = pe.matmul(s[:, c:c + n], qkt[rows, qtile, qt * P:(qt + 1) * P], qkt[rows, ktile, 0:n],
                              start=True, stop=True)
            m.then_inc(s_ready, 1)

        def turn_probs(pe, first, base, u):
            pe.wait_ge(e_ready, base + u + 1)
            s = set_of(first, u)
            for j in range(width_of(first, u) // P):
                m = pe.transpose(s[:, j * P:(j + 1) * P], ebuf[u % 3][:, j * P:(j + 1) * P], ident[:, :])
            m.then_inc(pt_ready, 1)

        def outputs(pe, first, base, u):
            pe.wait_ge(pt_out, base + u + 1)
            if u >= 2:
                pe.wait_ge(o_out, base + u - 1)
            o, pt, qt = ps[:, 6 + u % 2, :], ptb[u % 2], u % TT
            nk = qt + 1 if first else TT
            if u < UNITS // 2:
                h = u // TT
                if first:
                    rows = [(o[:, 0:HD], [(g * nk + k, proj[:, k, V1 + (4 * g + h) * HD:V1 + (4 * g + h + 1) * HD])
                                          for g in range(DIL_G) for k in range(nk)])]
                else:
                    rows = [(o[:, r * 2 * HD:(r + 1) * 2 * HD],
                             [(r * nk + k, proj[:, k, DV2 + h * 2 * HD:DV2 + (h + 1) * 2 * HD]) for k in range(nk)])
                            for r in range(2)]
            else:
                v = VB1 if first else SV2
                rows = [(o[:, r * HD:(r + 1) * HD],
                         [(r * nk + k, proj[:, k, v + r * HD:v + (r + 1) * HD]) for k in range(nk)]) for r in range(KV)]
            for dst, terms in rows:
                for i, (j, v) in enumerate(terms):
                    m = pe.matmul(dst, pt[:, j * P:(j + 1) * P], v, start=i == 0, stop=i == len(terms) - 1)
            m.then_inc(o_ready, 1)

        def hid_tile_pe(pe, g, par, t, ffn):
            pe.wait_ge(hid_ready, 2 * g + t + 1)
            for k in range((FFN_H if ffn else BW) // P):
                m = pe.transpose(ps[:, 2 * par + t, k * P:(k + 1) * P], hid_b[:, t, k * P:(k + 1) * P], ident[:, :])
            m.then_inc(hid_tr, 1)

        def hid_tr_pe(pe, g, par, ffn):
            for t in range(TT):
                hid_tile_pe(pe, g, par, t, ffn)

        def ffn_in_chunk(pe, t, par, slot, between=None):
            pe.wait_ge(lo_done[slot], t + 1)
            for b in range(4):
                k = 4 * slot + b
                m = block_mm(pe, xt_hi, xt_lo, k, slot, b, pair(par), k == 0, k == KD - 1)
                if b == 3:
                    m.then_inc(used[slot], 1)
                if b == 1 and between is not None:
                    between()

        def last_in_chunk(pe, t, par):
            pe.wait_ge(lo_done[1], t + 1)
            for i in range(TT):
                for b in range(4):
                    m = tile_mm(pe, xt_hi, xt_lo, 4 + b, 1, b, i, 2 * par + i, False, b == 3)
                m.then_inc(in_tile0 if i == 0 else used[1], 1)

        def down(pe, t, slots, g, first, last):
            pe.wait_ge(ht_lo_done, 2 * g + 2)
            for slot, ks in slots:
                pe.wait_ge(lo_done[slot], t + 1)
                for i, k in enumerate(ks):
                    for h in range(2):
                        m = block_mm(pe, ht_hi, ht_lo, k, slot, 2 * i + h, (4 + h, 6 + h), first and k == 0,
                                     last and slot == slots[-1][0] and k == slots[-1][1][-1])
                m.then_inc(used[slot], 1)

        def last_down(pe, t, slots, g, par, ffn):
            hid_tile_pe(pe, g, par, 0, ffn)
            for i in range(TT):
                pe.wait_ge(ht_lo_done, 2 * g + i + 1)
                for slot, ks in slots:
                    if i == 0:
                        pe.wait_ge(lo_done[slot], t + 1)
                    for j, k in enumerate(ks):
                        for h in range(2):
                            m = tile_mm(pe, ht_hi, ht_lo, k, slot, 2 * j + h, i, 4 + 2 * i + h, False, k == slots[-1][1][-1])
                        if i == 0 and j == 0 and slot == slots[0][0]:
                            hid_tile_pe(pe, g, par, 1, ffn)
                    if i == 1:
                        m.then_inc(used[slot], 1)
                if i == 0:
                    m.then_inc(y_tile0, 1)

        FFN_DOWN = ((2, (0, 1)),)
        MLP_DOWN = ((0, (0, 1)), (1, (2,)), (2, (3,)))

        def ffn_pe(pe, t, g, n):
            def step(s, par, first=False):
                ffn_in_chunk(pe, t + s, par, 0, lambda: hid_tr_pe(pe, g + s - 1, 1 - par, True))
                ffn_in_chunk(pe, t + s, par, 1)
                down(pe, t + s - 1, FFN_DOWN, g + s - 1, first, False)
            first_strip(pe, n, xres, t, (4, 4))
            step(1, 1, True)
            step(2, 0)
            with pe.Fori(3, FFN_S - 2, 2) as s:
                step(s, 1)
                step(s + 1, 0)
            step(FFN_S - 2, 1)
            ffn_in_chunk(pe, t + FFN_S - 1, 0, 0, lambda: hid_tr_pe(pe, g + FFN_S - 2, 1, True))
            down(pe, t + FFN_S - 2, FFN_DOWN, g + FFN_S - 2, False, False)
            last_in_chunk(pe, t + FFN_S - 1, 0)
            last_down(pe, t + FFN_S - 1, FFN_DOWN, g + FFN_S - 1, 0, True)

        @block.tensor
        def _(pe):
            pe.wait_ge(ident_ready, 1)
            first_strip(pe, 0, normed, 0, STRIP)
            strip(pe, 1, pair(1))
            with pe.Fori(2, S1_GATES, 2) as s:
                for par in range(2):
                    pe.wait_ge(proj_out, 2 * (s + par) - 2)
                    strip(pe, s + par, pair(par))
            pe.wait_ge(proj_out, 2 * (S1_GATES - 1))
            strip(pe, S1_GATES, pair(0))
            pe.wait_ge(roped, 2)
            qk_pe(pe, 0, range(6), 6, 2, qk_src1, QK1_TILES)
            blocks, _, _ = gate_plan()
            pe.wait_ge(proj_out, 2 * S1_GATES)
            for i in range(UNITS + 2):
                if i == 0:
                    pe.wait_ge(qk_out, 6)
                if i == UNITS // 2:
                    pe.wait_ge(roped, 4)
                    pe.wait_ge(o_out, i - 2)
                    qk_pe(pe, 0, range(6, QK1_BANKS), 6, 2, qk_src1, QK1_TILES)
                    pe.wait_ge(qk_out, QK1_BANKS)
                if i < UNITS:
                    scores(pe, True, 0, i)
                if 1 <= i <= UNITS:
                    turn_probs(pe, True, 0, i - 1)
                if i >= 2:
                    outputs(pe, True, 0, i - 2)
                for b in blocks[i]:
                    s = S1_SOLID + b // KD
                    if b % KD == 0:
                        pe.wait_ge(proj_out, 2 * s)
                    strip_block(pe, s, b % KD, pair(0))
            xt_pe(pe, 1, heads_out, 6)
            for slot in range(3):
                pe.wait_ge(lo_done[slot], T_BRANCH + 1)
                for k in range(2):
                    for h in range(2):
                        banks = (h, 2 + h) if slot == 0 else (4 + h, 6 + h)
                        m = block_mm(pe, xt_hi, xt_lo, 2 * slot + k, slot, 2 * k + h, banks,
                                     k == 0 and slot < 2, k == 1 and slot != 1)
                m.then_inc(used[slot], 1)
            first_strip(pe, 2, mixed, T_WOUT1, STRIP)
            last_strip(pe, T_WOUT1 + 1, 2)

            def step(s, par, first=False):
                strip(pe, mlp_up(s), pair(par), between=lambda: hid_tr_pe(pe, s - 1, 1 - par, False))
                down(pe, T_MLP + 2 * s, MLP_DOWN, s - 1, first, False)
            first_strip(pe, 3, normed, T_MLP, STRIP)
            step(1, 1, True)
            with pe.Fori(2, MLP_S, 2) as s:
                step(s, 0)
                step(s + 1, 1)
            last_down(pe, T_LAYER - 1, MLP_DOWN, MLP_S - 1, 1, False)
            with pe.Fori(0, LAYERS) as l:
                t, g, n = T_LAYER + L_TRIPLES * l, MLP_S + 2 * FFN_S * l, XT1 * (l + 1)
                base, qk = UNITS * (l + 1), QK1_BANKS + QK2_BANKS * l
                ffn_pe(pe, t, g, n)
                out0 = 2 * (S1 + S2 * l)

                def turn(events, heads):
                    pe.wait_ge(roped, 4 * (l + 1) + heads)
                    qk_pe(pe, qk, events, 4, 3, qk_src2, QK2_TILES)

                for j in range(S2):
                    if j >= 2:
                        pe.wait_ge(proj_out, out0 + 2 * (j - 1))
                    if j == 0:
                        first_strip(pe, n + 1, xres, t + L_PROJ, STRIP)
                        continue
                    strip(pe, t + L_PROJ + j, pair(j % 2), PROJ2[j][1],
                          between=(lambda: turn((4, 5, 6), 4)) if j == S2 - 1 else None, at=5)
                    if j == 1:
                        turn((0, 1), 1)
                    if j == 2:
                        turn((2, 3), 2)
                pe.wait_ge(qk_out, qk + QK2_BANKS)
                pe.wait_ge(proj_out, out0 + 2 * S2)
                for i in range(UNITS + 2):
                    if i >= 2:
                        turn_probs(pe, False, base, i - 2)
                    if i < UNITS:
                        scores(pe, False, base, i)
                    if i >= 2:
                        outputs(pe, False, base, i - 2)
                first_strip(pe, n + 2, heads_out, t + L_WOUT, STRIP)
                last_strip(pe, t + L_WOUT + 1, 2)
                ffn_pe(pe, t + L_FFN2, g + FFN_S, n + 3)


_INS = ['x', 'positions', 'ln1_g', 'w_in', 'q_norm_a', 'k_norm_a', 'q_norm_b', 'k_norm_b', 'sinks', 'w_branch_a',
        'w_branch_b', 'w_out', 'ln2_g', 'w_up', 'w_down', 'positions_2', 'w_in_2', 'w_out_2', 'diff_lambda_2',
        'diff_subln_g_2', 'swa_sink_2', 'ffn1_w_in_2', 'ffn1_w_out_2', 'ffn2_w_in_2', 'ffn2_w_out_2', 'ln_g_2',
        'ln_b_2']


def kernel(**inputs):
    import concourse.bacc as _bacc
    from concourse.bass_utils import run_bass_kernel_spmd as _run

    nc = _bacc.Bacc("TRN2", target_bir_lowering=False, num_devices=1)
    arrays, args = {}, []
    for name in _INS:
        a = np.ascontiguousarray(inputs[name])
        arrays[f"in_{name}_dram"] = a
        args.append(nc.dram_tensor(f"in_{name}_dram", a.shape, mybir.dt.from_np(a.dtype), kind="ExternalInput").ap())
    args.append(nc.dram_tensor("out_0_dram", (1, TOK, DM), F32, kind="ExternalOutput").ap())
    build(nc, *args)
    r = _run(nc, [arrays], core_ids=[0])
    return r.results[0]["out_0_dram"]
```

```python
import math
from contextlib import ExitStack

import numpy as np
import concourse.bass as bass
from concourse import mybir

P = 128
TOK = 256
TT = TOK // P
DM = 1024
KD = DM // P
HD = 64
N1 = 5120
DIL_W = 768
DIL_G, DIL_SLOTS = 3, 4
V1, QB1, KB1, VB1, QKV1 = 2 * DIL_W, 3 * DIL_W, 3 * DIL_W + 512, 3 * DIL_W + 640, 3 * DIL_W + 768
OA_W = DIL_SLOTS * HD
FF1 = 4 * DM
DK2, DV2, SQ2, SK2, SV2 = 512, 1024, 1536, 2048, 2176
FF2 = 2816
LAYERS = 2
KV = 2
ALPHA = (2.0 * LAYERS) ** 0.25
EPS1, EPS2 = 1e-6, 1e-5
LAMBDA_INIT = [0.8 - 0.6 * math.exp(-0.3 * l) for l in range(LAYERS)]
SCALE = HD ** -0.5
NEG = -1e30
ROPE1, ROPE2 = 8, 32
ROPES = ROPE1 + ROPE2
INV_FREQ = [float(v) for v in np.concatenate([
    np.float32(500000.0) ** (-np.arange(0, 16, 2, dtype=np.float32) / np.float32(16)),
    np.float32(10000.0) ** (-np.arange(0, 64, 2, dtype=np.float32) / np.float32(64))]).astype(np.float32)]
TWO_PI = (6.28125, 1.9350051879882812e-3, 3.0199159819567528e-7)
ROUND = 1.5 * 2.0 ** 23
PI_LOW = 3.1415925

SLOTS = 3
BW = 512
STRIP = (3, 3, 2)
S1 = N1 // BW
S1_GATES = QKV1 // BW
S1_SOLID = 7
STEP_BLOCKS = (1, 1, 1, 1, 1, 1, 1, 1, 1, 1, 2, 2, 2, 2, 2, 2, 2, 0)
NORMS = ((24, 0), (24, 0), (10, QB1), (10, QB1))
MLP_S = FF1 // BW
FFN_H = BW // 2
FFN_S = FF2 // FFN_H
PROJ2 = ((0, BW), (DK2, BW), (SQ2, BW), (SK2, 2 * KV * HD), (DV2, BW))
S2 = len(PROJ2)
T_BRANCH = S1
T_WOUT1 = T_BRANCH + 1
T_MLP = T_WOUT1 + 2
T_LAYER = T_MLP + 2 * MLP_S
L_PROJ = FFN_S
L_WOUT = L_PROJ + S2
L_FFN2 = L_WOUT + 2
L_TRIPLES = L_FFN2 + FFN_S
Y_PARTS = 7
UNITS = 16
XT1 = 4
QK1_TILES, QK2_TILES = 17, 13
QK1_BANKS, QK2_BANKS = 9, 7

F32 = mybir.dt.float32
F32R = mybir.dt.float32r
BF16 = mybir.dt.bfloat16
I32 = mybir.dt.int32
ALU = mybir.AluOpType
ACT = mybir.ActivationFunctionType
AX = mybir.AxisListType


def build(nc, x, positions, ln1_g, w_in, q_norm_a, k_norm_a, q_norm_b, k_norm_b, sinks, w_branch_a,
          w_branch_b, w_out, ln2_g, w_up, w_down, positions_2, w_in_2, w_out_2, diff_lambda_2,
          diff_subln_g_2, swa_sink_2, ffn1_w_in_2, ffn1_w_out_2, ffn2_w_in_2, ffn2_w_out_2,
          ln_g_2, ln_b_2, out):
    ds = bass.ds
    w_in_r = w_in[0].rearrange("(k p) n -> p k n", p=P)
    wa_r = w_branch_a[0].rearrange("(k p) n -> p k n", p=P)
    wb_r = w_branch_b[0].rearrange("(k p) n -> p k n", p=P)
    w_out_r = w_out[0].rearrange("(k p) n -> p k n", p=P)
    w_up_r = w_up[0].rearrange("(k p) n -> p k n", p=P)
    w_down_r = w_down[0].rearrange("(s k p) n -> s p k n", p=P, k=BW // P)
    w_in2_r = w_in_2.rearrange("l (k p) n -> l p k n", p=P)
    w_out2_r = w_out_2.rearrange("l (k p) n -> l p k n", p=P)
    ffn_in_r = [w.rearrange("l (k p) n -> l p k n", p=P) for w in (ffn1_w_in_2, ffn2_w_in_2)]
    ffn_out_r = [w.rearrange("l (s k p) n -> l s p k n", p=P, k=FFN_H // P) for w in (ffn1_w_out_2, ffn2_w_out_2)]
    x_r = x[0].rearrange("(t p) n -> p t n", p=P)
    out_r = out[0].rearrange("(t p) n -> p t n", p=P)

    ctx = ExitStack()
    with ctx:
        def sb(name, shape, dt=F32):
            return ctx.enter_context(nc.sbuf_tensor(name, shape, dt))

        def sem(name):
            return ctx.enter_context(nc.semaphore(name))

        raw = [sb(f"raw{j}", [P, 4, BW]) for j in range(SLOTS)]
        whi = [sb(f"whi{j}", [P, 4, BW], F32R) for j in range(SLOTS)]
        wlo = [sb(f"wlo{j}", [P, 4, BW], F32R) for j in range(SLOTS)]
        xres = sb("xres", [P, TT, DM])
        xt_hi = sb("xt_hi", [P, KD, TOK], F32R)
        xt_lo = sb("xt_lo", [P, KD, TOK], F32R)
        ht_hi = sb("ht_hi", [P, BW // P, TOK], F32R)
        ht_lo = sb("ht_lo", [P, BW // P, TOK], F32R)
        proj = sb("proj", [P, TT, QKV1])
        gates = sb("gates", [P, TT, 2 * DM])
        qkt = sb("qkt", [P, QK1_TILES, TOK])
        ebuf = [sb(f"ebuf{j}", [P, 3 * TOK]) for j in range(3)]
        ptb = [sb(f"ptb{j}", [P, 3 * TOK]) for j in range(2)]
        square = sb("square", [P, 2 * DIL_W])
        ln_g = sb("ln_g", [P, DM])
        ln_b = sb("ln_b", [P, DM])
        mask = sb("mask", [P, 6, TOK], BF16)
        ident = sb("ident", [P, P])
        dist = sb("dist", [P, P], I32)
        dist4 = sb("dist4", [P, 2, P], I32)
        gain = sb("gain", [P, 4, HD])
        pos_i = sb("pos_i", [P, 2, TT], I32)
        pos_f = sb("pos_f", [P, 2, TT])
        inv = sb("inv", [P, ROPES])
        ang = sb("ang", [P, TT, ROPES])
        turns = sb("turns", [P, TT, ROPES])
        part = sb("part", [P, TT, ROPES])
        cosb = sb("cosb", [P, TT, ROPES])
        sinb = sb("sinb", [P, TT, ROPES])
        rope = sb("rope", [P, 4, 8 * ROPE2])
        half = sb("half", [P, 24])
        ln_eps = sb("ln_eps", [P, 1])
        per_head = sb("per_head", [P, 1])
        ssum = sb("ssum", [P, 24])
        rstd = sb("rstd", [P, 24])
        stats = sb("stats", [P, TT, 2, 6])
        mv = sb("mv", [P, TT, 2])
        lrs = sb("lrs", [P, TT])
        top = sb("top", [P, 4, 2])
        ntop = sb("ntop", [P, 4, 2])
        nsink = sb("nsink", [P, 4, 2])
        scratch = sb("scratch", [P, 1])
        esink = sb("esink", [P, 4, 2])
        den = sb("den", [P, 4, 2])
        rden = sb("rden", [P, 4, 2])
        sink1 = sb("sink1", [P, 8])
        sink2 = sb("sink2", [P, LAYERS, 8])
        sinkc = sb("sinkc", [P, 8])
        dlam = sb("dlam", [P, LAYERS, 4, HD])
        dprod = sb("dprod", [P, LAYERS, 2, HD])
        dsum = sb("dsum", [P, LAYERS, 2])
        dexp = sb("dexp", [P, LAYERS, 2])
        lam = sb("lam", [P, LAYERS])
        second = sb("second", [P, 2 * HD])
        lamc = sb("lamc", [P, 1])
        subg = sb("subg", [P, LAYERS, 2 * HD])
        subgc = sb("subgc", [P, 2 * HD])
        dss = sb("dss", [P, TT * 4])
        drs = sb("drs", [P, TT * 4])
        rope1 = square[:, 0:4 * 8 * ROPE2].rearrange("p (j n) -> p j n", j=4)
        normed = proj[:, :, 0:DM]
        hid_a = proj[:, :, 0:BW]
        hid_b = proj[:, :, BW:2 * BW]
        heads_out = proj[:, :, 0:DM]
        mixed = proj[:, :, DM:2 * DM]
        mix_b = proj[:, :, 2 * DM:3 * DM]
        ps = ctx.enter_context(nc.psum_tensor("ps", [P, 8, BW], F32))

        loaded = [sem(f"loaded{j}") for j in range(SLOTS)]
        hi_done = [sem(f"hi_done{j}") for j in range(SLOTS)]
        lo_done = [sem(f"lo_done{j}") for j in range(SLOTS)]
        hi_half = sem("hi_half")
        lo_half = sem("lo_half")
        lo_first = sem("lo_first")
        used = [sem(f"used{j}") for j in range(SLOTS)]
        x_loaded = [sem(f"x_loaded{t}") for t in range(TT)]
        const_loaded = sem("const_loaded")
        g_loaded = sem("g_loaded")
        ident_ready = sem("ident_ready")
        mask_pool = sem("mask_pool")
        mask_mod = sem("mask_mod")
        consts_set = sem("consts_set")
        ang_ready = sem("ang_ready")
        trig_ready = sem("trig_ready")
        lam_sum = sem("lam_sum")
        lam_exp = sem("lam_exp")
        rms_sum = sem("rms_sum")
        rms_rstd = sem("rms_rstd")
        xt_src = sem("xt_src")
        xt_tr = sem("xt_tr")
        xt_hi_done = sem("xt_hi_done")
        xt_lo_done = sem("xt_lo_done")
        proj_out = sem("proj_out")
        gate_half = sem("gate_half")
        head_sq = sem("head_sq")
        head_ss = sem("head_ss")
        head_rstd = sem("head_rstd")
        roped = sem("roped")
        roped1 = sem("roped1")
        qk_tr = sem("qk_tr")
        qk_out = sem("qk_out")
        s_ready = sem("s_ready")
        top_ready = sem("top_ready")
        e_ready = sem("e_ready")
        esink_ready = sem("esink_ready")
        pt_ready = sem("pt_ready")
        pt_out = sem("pt_out")
        o_ready = sem("o_ready")
        o_out = sem("o_out")
        dsq = sem("dsq")
        dsum_ready = sem("dsum_ready")
        heads_normed = sem("heads_normed")
        hid_act = sem("hid_act")
        hid_ready = sem("hid_ready")
        hid_tr = sem("hid_tr")
        branch_tile0 = sem("branch_tile0")
        in_tile0 = sem("in_tile0")
        y_part = sem("y_part")
        ht_hi_done = sem("ht_hi_done")
        ht_lo_done = sem("ht_lo_done")
        res_ready = sem("res_ready")
        var_ready = sem("var_ready")
        lrs_ready = sem("lrs_ready")
        stored = sem("stored")

        def mlp_up(s):
            return T_MLP if isinstance(s, int) and s == 0 else T_MLP + 2 * s - 1


        def load(sp, slot, t, dst, src, inc=32, layers=None):
            if not isinstance(t, int) or t > 0:
                sp.wait_ge(lo_done[slot], t)
            if layers is not None:
                sp.wait_ge(lo_first, layers)
            sp.dma_start(dst, src).then_inc(loaded[slot], inc)

        def load_strip(sp, t, w, col, width):
            k = 0
            for j, n in enumerate(STRIP):
                load(sp, j, t, raw[j][:, 0:n, 0:width], w[:, k:k + n, ds(col, width)])
                k += n

        def load_ffn_in(sp, t, w, l, s, layers=None):
            for j in range(2):
                load(sp, j, t, raw[j][:, :, FFN_H:BW], w[l, :, 4 * j:4 * j + 4, ds(s * FFN_H + FF2, FFN_H)], 16,
                     layers if j == 0 else None)
                sp.dma_start(raw[j][:, :, 0:FFN_H], w[l, :, 4 * j:4 * j + 4, ds(s * FFN_H, FFN_H)]).then_inc(loaded[j], 16)

        def load_ffn_out(sp, t, w, l, s):
            load(sp, 2, t, raw[2][:, :, :].rearrange("p (k h) n -> p k (h n)", h=2), w[l, s, :, :, :])

        def load_down(sp, t, s):
            k = 0
            for j, n in enumerate((2, 1, 1)):
                load(sp, j, t, raw[j][:, 0:2 * n, :].rearrange("p (k h) n -> p k (h n)", h=2),
                     w_down_r[s, :, k:k + n, :])
                k += n

        def load_ln(sp, l, j):
            n = XT1 * (l + 1) + (0, 1, 3)[j]
            sp.wait_ge(xt_src, 4 * n + 4)
            sp.dma_start(ln_g[:, :], ln_g_2[l, j, :].partition_broadcast(P)).then_inc(g_loaded, 16)
            sp.dma_start(ln_b[:, :], ln_b_2[l, j, :].partition_broadcast(P)).then_inc(g_loaded, 16)

        def load_ffn(sp, t, f, l, layers):
            wi, wo = ffn_in_r[f], ffn_out_r[f]
            load_ffn_in(sp, t + 1, wi, l, 1, layers)
            load_ffn_out(sp, t, wo, l, 0)
            load_ffn_in(sp, t + 2, wi, l, 2)
            load_ffn_out(sp, t + 1, wo, l, 1)
            load_ln(sp, l, 2 * f)
            with sp.Fori(3, FFN_S) as s:
                load_ffn_in(sp, t + s, wi, l, s)
                load_ffn_out(sp, t + s - 1, wo, l, s - 1)

        def load_strip2(sp, t, l, j, slots):
            col, width = PROJ2[j]
            for q in slots:
                k = sum(STRIP[:q])
                load(sp, q, t, raw[q][:, 0:STRIP[q], 0:width], w_in2_r[l, :, k:k + STRIP[q], col:col + width])

        block = ctx.enter_context(nc.Block())

        @block.sync
        def _(sp):
            for t in range(TT):
                sp.dma_start(xres[:, t, :], x_r[:, t, :]).then_inc(x_loaded[t], 16)
            sp.dma_start(ln_g[:, :], ln1_g[0, :].partition_broadcast(P)).then_inc(g_loaded, 16)
            load_strip(sp, 0, w_in_r, 0, BW)
            with sp.Fori(1, S1) as s:
                load_strip(sp, s, w_in_r, s * BW, BW)
            load(sp, 0, T_BRANCH, raw[0][:, :, :].rearrange("p (k h) n -> p k (h n)", h=2), wa_r[:, 0:2, :])
            for j in (1, 2):
                load(sp, j, T_BRANCH, raw[j][:, :, :].rearrange("p (k h) n -> p k (h n)", h=2),
                     wb_r[:, 2 * j - 2:2 * j, :])
            for s in range(2):
                load_strip(sp, T_WOUT1 + s, w_out_r, s * BW, BW)
            sp.wait_ge(xt_src, 4)
            sp.dma_start(ln_g[:, :], ln2_g[0, :].partition_broadcast(P)).then_inc(g_loaded, 16)
            load_strip(sp, T_MLP, w_up_r, 0, BW)
            with sp.Fori(1, MLP_S) as s:
                load_strip(sp, T_MLP - 1 + s * 2, w_up_r, s * BW, BW)
                load_down(sp, T_MLP + s * 2, s - 1)
            load_down(sp, T_LAYER - 1, MLP_S - 1)
            load_ffn_in(sp, T_LAYER, ffn_in_r[0], 0, 0)
            with sp.Fori(0, LAYERS) as l:
                t = T_LAYER + L_TRIPLES * l
                layers = sp.snap(l + 1)
                load_ffn(sp, t, 0, l, None)
                load_strip2(sp, t + L_PROJ, l, 0, (0, 1))
                load_ffn_out(sp, t + FFN_S - 1, ffn_out_r[0], l, FFN_S - 1)
                load_strip2(sp, t + L_PROJ, l, 0, (2,))
                for j in range(1, S2):
                    load_strip2(sp, t + L_PROJ + j, l, j, (0, 1, 2))
                load_ln(sp, l, 1)
                for s in range(2):
                    load_strip(sp, t + L_WOUT + s, w_out2_r[l], s * BW, BW)
                load_ffn_in(sp, t + L_FFN2, ffn_in_r[1], l, 0)
                load_ffn(sp, t + L_FFN2, 1, l, layers)
                load_ffn_in(sp, t + L_TRIPLES, ffn_in_r[0], LAYERS - 1, 0)
                load_ffn_out(sp, t + L_FFN2 + FFN_S - 1, ffn_out_r[1], l, FFN_S - 1)
            for t in range(TT):
                for h in range(2):
                    cols = slice(h * BW, (h + 1) * BW)
                    sp.wait_ge(xt_src, 4 * (XT1 + XT1 * LAYERS) + 2 * t + h + 1)
                    sp.dma_start(out_r[:, t, cols], xres[:, t, cols]).then_inc(stored, 16)
            sp.wait_ge(stored, 32 * TT)


        def split_hi(act, slot, t, n, width=BW):
            act.wait_ge(loaded[slot], 32 * (t + 1))
            if not isinstance(t, int) or t > 0:
                act.wait_ge(used[slot], t)
            act.activation(whi[slot][:, 0:n, 0:width], raw[slot][:, 0:n, 0:width], ACT.Copy).then_inc(hi_done[slot], 1)

        def split_hi_halves(act, slot, t):
            act.wait_ge(loaded[slot], 32 * (t + 1))
            act.wait_ge(used[slot], t)
            for h in range(2):
                act.activation(whi[slot][:, 2 * h:2 * h + 2, :], raw[slot][:, 2 * h:2 * h + 2, :],
                               ACT.Copy).then_inc(hi_half if h == 0 else hi_done[slot], 1)

        def split_lo_halves(dve, slot, t, part):
            for h in range(2):
                if h == 0:
                    dve.wait_ge(hi_half, part)
                else:
                    dve.wait_ge(hi_done[slot], t + 1)
                dve.tensor_tensor(wlo[slot][:, 2 * h:2 * h + 2, :], raw[slot][:, 2 * h:2 * h + 2, :],
                                  whi[slot][:, 2 * h:2 * h + 2, :].bitcast(F32),
                                  ALU.subtract).then_inc(lo_half if h == 0 else lo_done[slot], 1)

        def split_lo(dve, slot, t, n, width=BW):
            dve.wait_ge(hi_done[slot], t + 1)
            dve.tensor_tensor(wlo[slot][:, 0:n, 0:width], raw[slot][:, 0:n, 0:width],
                              whi[slot][:, 0:n, 0:width].bitcast(F32), ALU.subtract).then_inc(lo_done[slot], 1)

        def rotate(eng, x1, x2, cos, sin, t1, t2, t3, t4):
            eng.tensor_tensor(t1, x1, cos, ALU.mult)
            eng.tensor_tensor(t2, x2, sin, ALU.mult)
            eng.tensor_tensor(t3, x2, cos, ALU.mult)
            eng.tensor_tensor(t4, x1, sin, ALU.mult)
            eng.drain()
            eng.tensor_tensor(x1, t1, t2, ALU.subtract)
            return eng.tensor_tensor(x2, t3, t4, ALU.add)

        def rotate_strip(eng, l, j, t, tmp, done):
            col = PROJ2[j][0]
            heads = 2 if col == SK2 else 8
            eng.drain()
            eng.wait_ge(proj_out, 2 * (S1 + S2 * l + j) + t + 1)
            v = proj[:, t, col:col + heads * HD].rearrange("p (h r d) -> p h r d", r=2, d=ROPE2)
            tmp = [tmp[:, i, 0:heads * ROPE2].rearrange("p (h d) -> p h d", d=ROPE2) for i in range(4)]
            c, s = (z[:, t:t + 1, ROPE1:ROPES].to_broadcast([P, heads, ROPE2]) for z in (cosb, sinb))
            rotate(eng, v[:, :, 0, :], v[:, :, 1, :], c, s, *tmp).then_inc(done, 1)

        def rsqrt(pool, dst, src, scale, eps, done):
            pool.tensor_scalar(dst, src, scale, eps, ALU.mult, ALU.add)
            pool.drain()
            pool.tensor_tensor(dst, dst, half[:, 0:dst.shape[-1]], ALU.pow).then_inc(done, 1)

        def norm_pool(pool, q, T, n, last=False, mix=None):
            for t in range(TT):
                pool.wait_ge(var_ready, 2 * q + t + 1)
                pool.tensor_tensor(lrs[:, t:t + 1], mv[:, t, 1:2], ln_eps[:, :], ALU.add)
                pool.drain()
                pool.tensor_tensor(lrs[:, t:t + 1], lrs[:, t:t + 1], half[:, 0:1], ALU.pow).then_inc(lrs_ready, 1)
                if t == 0 and mix is not None:
                    pool.wait_ge(hi_done[0], T + 1)
                    pool.tensor_tensor(wlo[0][:, 2:4, :], raw[0][:, 2:4, :], whi[0][:, 2:4, :].bitcast(F32),
                                       ALU.subtract).then_inc(lo_done[0], 1)
                if t == 0:
                    split_lo(pool, 1, T, n)
                if t == 0 and last:
                    split_lo(pool, 2, T, STRIP[2])

        def rms_pool(pool, i, toks=range(TT)):
            for t in toks:
                pool.wait_ge(rms_sum, 2 * i + t + 1)
                rsqrt(pool, lrs[:, t:t + 1], mv[:, t, 1:2], 1.0 / DM, EPS1, rms_rstd)

        @block.gpsimd
        def _(pool):
            pool.memset(half[:, :], -0.5)
            pool.memset(ln_eps[:, :], EPS2 / ALPHA ** 2)
            pool.memset(per_head[:, :], 1.0 / (2 * HD))
            pool.memset(ident[:, :], 0.0)
            pool.drain()
            pool.affine_select(out=ident[:, :], in_=ident[:, :], compare_op=ALU.not_equal, fill=1.0,
                               base=0, pattern=[[-1, P]], channel_multiplier=1).then_inc(ident_ready, 1)
            rms_pool(pool, 0)
            with nc.allow_non_contiguous_dma(reason="positions, one to a partition"):
                pool.dma_start(pos_i[:, 0, :], positions.rearrange("a (t p) -> p (a t)", p=P)).then_inc(const_loaded, 16)
                pool.dma_start(pos_i[:, 1, :], positions_2.rearrange("a (t p) -> p (a t)", p=P)).then_inc(const_loaded, 16)
            for j, g in enumerate((q_norm_a, k_norm_a, q_norm_b, k_norm_b)):
                pool.dma_start(gain[:, j, :], g[0, :].partition_broadcast(P)).then_inc(const_loaded, 16)
            pool.dma_start(sink1[:, :], sinks[0, :].partition_broadcast(P)).then_inc(const_loaded, 16)
            pool.dma_start(sink2[:, :, :], swa_sink_2.partition_broadcast(P)).then_inc(const_loaded, 16)
            pool.dma_start(subg[:, :, :], diff_subln_g_2.partition_broadcast(P)).then_inc(const_loaded, 16)
            pool.dma_start(dlam[:, :, :, :], diff_lambda_2.partition_broadcast(P)).then_inc(const_loaded, 16)
            for j, f in enumerate(INV_FREQ):
                pool.memset(inv[:, j:j + 1], f)
            pool.memset(mask[:, :, :], 0.0)
            pool.iota(dist[:, :], [[1, P]], base=P, channel_multiplier=-1).then_inc(consts_set, 1)
            pool.drain()
            pool.wait_ge(mask_mod, 1)
            for kind in range(5):
                pool.affine_select(out=mask[:, kind, P:TOK], in_=mask[:, kind, P:TOK], compare_op=ALU.is_ge,
                                   fill=NEG, base=0, pattern=[[-1, P]], channel_multiplier=1)
            for kind, least in ((0, 0), (5, 0), (3, 1)):
                pool.affine_select(out=mask[:, kind, 0:P], in_=mask[:, kind, 0:P], compare_op=ALU.is_ge,
                                   fill=NEG, base=-least, pattern=[[1, P]], channel_multiplier=-1)
            pool.drain().then_inc(mask_pool, 1)
            for i, (heads, _) in enumerate(NORMS):
                pool.wait_ge(head_ss, i + 1)
                rsqrt(pool, rstd[:, 0:heads], ssum[:, 0:heads], 1.0 / HD, EPS1, head_rstd)
            for s in range(S1_GATES, S1):
                pool.wait_ge(proj_out, 2 * s + 2)
                g = gates[:, :, (s - S1_GATES) * BW:(s - S1_GATES + 1) * BW]
                pool.tensor_scalar(g, g, 0.5, 0.5, ALU.mult, ALU.add).then_inc(gate_half, 1)
            rms_pool(pool, 1, (0,))
            split_lo(pool, 1, T_MLP, STRIP[1])
            rms_pool(pool, 1, (1,))
            with pool.Fori(0, LAYERS) as l:
                q = 3 * l
                norm_pool(pool, q, T_LAYER + L_TRIPLES * l + L_PROJ, STRIP[1], True)
                for j in range(S2 - 1):
                    rotate_strip(pool, l, j, 1, rope1, roped1)
                split_lo(pool, 2, T_LAYER + L_TRIPLES * l + L_WOUT, STRIP[2])
                pool.wait_ge(o_out, UNITS * (l + 1) + UNITS // 2)
                pool.tensor_tensor(square[:, 0:TT * BW].rearrange("p (t n) -> p t n", t=TT), heads_out[:, :, 0:BW],
                                   heads_out[:, :, 0:BW], ALU.mult).then_inc(dsq, 1)
                pool.wait_ge(dsum_ready, l + 1)
                pool.tensor_tensor(drs[:, :], dss[:, :], per_head[:, :].to_broadcast([P, TT * 4]), ALU.mult)
                pool.drain()
                pool.tensor_scalar(drs[:, :], drs[:, :], 1.0, EPS2, ALU.mult, ALU.add)
                pool.drain()
                pool.tensor_tensor(drs[:, :], drs[:, :], half[:, 0:TT * 4], ALU.pow)
                for by in range(2):
                    pool.drain()
                    for k in range(TT):
                        v = heads_out[:, k, 0:BW].rearrange("p (h d) -> p h d", d=2 * HD)
                        m = pool.tensor_tensor(v, v, drs[:, 4 * k:4 * k + 4].unsqueeze(2).to_broadcast([P, 4, 2 * HD])
                                               if by == 0 else
                                               subgc[:, :].unsqueeze(1).to_broadcast([P, 4, 2 * HD]), ALU.mult)
                m.then_inc(heads_normed, 1)
                norm_pool(pool, q + 1, T_LAYER + L_TRIPLES * l + L_FFN2, 4, mix=l)
                norm_pool(pool, q + 2, T_LAYER + L_TRIPLES * (l + 1), 4)

        def gate_plan():
            blocks, at = [], 0
            for n in STEP_BLOCKS:
                blocks.append(range(at, at + n))
                at += n
            assert at == (S1 - S1_SOLID) * KD
            step_of = {b: i for i, r in enumerate(blocks) for b in r}
            ends = [step_of[s * KD + sum(STRIP[:j + 1]) - 1] for s in range(S1 - S1_SOLID) for j in range(SLOTS)]
            splits = {2: [(2, S1_SOLID, STRIP[2])]}
            for c in range(3, len(ends) + 3):
                s, j = S1_SOLID + c // 3, c % 3
                splits.setdefault(ends[c - 3] + 1, []).append((j, s, STRIP[j] if s < S1 else 4))
            reads = {ends[3 * s + 2] + 1: S1_SOLID + s for s in range(S1 - S1_SOLID)}
            return blocks, splits, reads

        def xt_act(act, n, tiles=KD, toks=range(TT)):
            for t in toks:
                for b in range(2):
                    m = min(4, tiles - 4 * b)
                    act.wait_ge(xt_tr, 4 * n + 2 * t + b + 1)
                    act.activation(xt_hi[:, 4 * b:4 * b + m, t * P:(t + 1) * P],
                                   ps[:, 2 * t + b, 0:m * P].rearrange("p (k n) -> p k n", k=m),
                                   ACT.Copy).then_inc(xt_hi_done, 1)

        def paired(ap, heads):
            return ap.rearrange("p (g r d) -> p r g d", r=KV, d=HD)[:, heads // 4]

        def read_strip(act, done, parts, banks, func=ACT.Copy, scale=1.0):
            act.wait_ge(used[2], done)
            for t in range(TT):
                for col, width, dst in parts:
                    src, d = ps[:, banks[t], col:col + width], dst(t)
                    if len(d.shape) == 3:
                        src = src.rearrange("p (g d) -> p g d", d=HD)
                    m = act.activation(d, src, func, scale=scale)
                m.then_inc(proj_out, 1)

        def read_proj1(act, s):
            c = s * BW
            plain = lambda a, z: (a, z - a, lambda t: proj[:, t, c + a:c + z])
            heads = lambda a, h: (a, 4 * HD, lambda t: paired(proj[:, t, QB1:QB1 + 8 * HD], h))
            if c < QB1 < c + BW:
                parts = [plain(0, QB1 - c), heads(QB1 - c, 0)]
            elif c < KB1 < c + BW:
                parts = [heads(0, 4), plain(KB1 - c, BW)]
            else:
                parts = [plain(0, BW)]
            read_strip(act, s + 1, parts, (2 * (s % 2), 2 * (s % 2) + 1))

        def read_gate(act, s):
            c = (s - S1_GATES) * BW
            read_strip(act, s + 1, [(0, BW, lambda t: gates[:, t, c:c + BW])], (0, 1), ACT.Tanh, 0.5)

        def read_proj2(act, t, j):
            col, width = PROJ2[j]
            if col == SQ2:
                parts = [(4 * r * HD, 4 * HD, lambda i, r=r: paired(proj[:, i, col:col + width], 4 * r)) for r in range(KV)]
            else:
                parts = [(0, width, lambda i: proj[:, i, col:col + width])]
            read_strip(act, t + L_PROJ + j + 1, parts, (2 * (j % 2), 2 * (j % 2) + 1))

        def read_qk(act, base, events, bank0, tiles, banks):
            for e in events:
                m = min(2, tiles - 2 * e)
                act.wait_ge(qk_tr, base + e + 1)
                act.activation(qkt[:, 2 * e:2 * e + m, :],
                               ps[:, bank0 + e % banks, 0:m * TOK].rearrange("p (k n) -> p k n", k=m),
                               ACT.Copy).then_inc(qk_out, 1)

        def set_of(first, u):
            b = 2 + 2 * (u % 2) if first else 2 * ((u + 2) % 3)
            return ps[:, b:b + 2, :].rearrange("p b n -> p (b n)")

        def width_of(first, u):
            if first and u < UNITS // 2:
                return DIL_G * P * (u % TT + 1)
            if first:
                return KV * P * (u % TT + 1)
            return 2 * TOK

        def exps(act, first, base, u):
            act.wait_ge(top_ready, base + u + 1)
            i = u % 4
            e = ebuf[u % 3]
            if u < UNITS // 2:
                if first:
                    w = width_of(first, u)
                    act.activation(e[:, 0:w], e[:, 0:w], ACT.Exp, bias=ntop[:, i, 0:1],
                                   accum_out=den[:, i, 0:1]).then_inc(e_ready, 1)
                    return
                for r in range(2):
                    o = act.activation(e[:, r * TOK:(r + 1) * TOK], set_of(first, u)[:, r * BW:r * BW + TOK],
                                       ACT.Exp, bias=ntop[:, i, r:r + 1], scale=SCALE, accum_out=den[:, i, r:r + 1])
                o.then_inc(e_ready, 1)
                return
            w = width_of(first, u) // KV
            for r in range(KV):
                o = act.activation(e[:, r * w:(r + 1) * w], e[:, r * w:(r + 1) * w], ACT.Exp,
                                   bias=ntop[:, i, r:r + 1], accum_out=den[:, i, r:r + 1])
            o.then_inc(e_ready, 1)
            g = (u - UNITS // 2) // TT
            for r in range(KV):
                o = act.activation(esink[:, i, r:r + 1], (sink1 if first else sinkc)[:, g + 4 * r:g + 4 * r + 1], ACT.Exp,
                                   bias=ntop[:, i, r:r + 1])
            o.then_inc(esink_ready, 1)

        def read_pt(act, first, base, u):
            w = width_of(first, u)
            act.wait_ge(pt_ready, base + u + 1)
            if u >= 2:
                act.wait_ge(o_ready, base + u - 1)
            act.activation(ptb[u % 2][:, 0:w], set_of(first, u)[:, 0:w], ACT.Copy).then_inc(pt_out, 1)

        def head_square(act, i):
            heads, col = NORMS[i]
            if i > 0:
                act.wait_ge(head_ss, i)
            act.drain()
            act.activation(square[:, 0:heads * HD], proj[:, i % 2, col:col + heads * HD], ACT.Square).then_inc(head_sq, 1)

        def rms_act(act, i, toks=range(TT)):
            for t in toks:
                if i > 0:
                    act.wait_ge(res_ready, t + 1)
                act.activation(normed[:, t, :], xres[:, t, :], ACT.Square,
                               accum_out=mv[:, t, 1:2]).then_inc(rms_sum, 1)

        def hidden_act(act, g, done, par, ffn, tile0=None, toks=range(TT)):
            w = FFN_H if ffn else BW
            for t in toks:
                if tile0 is not None and t == 0:
                    act.wait_ge(in_tile0, tile0)
                elif tile0 is not None or t == 0:
                    act.wait_ge(used[1 if ffn else 2], done)
                act.activation(hid_a[:, t, 0:w], ps[:, 2 * par + t, 0:w], ACT.Silu if ffn else ACT.Relu).then_inc(hid_act, 1)

        def ht_act(act, g, par, ffn, toks=range(TT)):
            k = (FFN_H if ffn else BW) // P
            for t in toks:
                act.wait_ge(hid_tr, 2 * g + t + 1)
                act.activation(ht_hi[:, 0:k, t * P:(t + 1) * P],
                               ps[:, 2 * par + t, 0:k * P].rearrange("p (k n) -> p k n", k=k), ACT.Copy).then_inc(ht_hi_done, 1)

        def ffn_act(act, t, g, f, after):
            def step(s, par, n=(4, 4), first=False):
                if not first:
                    hidden_act(act, g + s - 1, t + s, 1 - par, True)
                split_hi(act, 2, t + s - 1, 4)
                ht_act(act, g + s - 1, 1 - par, True)
                split_hi(act, 0, t + s + 1, n[0])
                split_hi(act, 1, t + s + 1, n[1])
            act.activation(scratch[:, :], ident[:, 0:1], ACT.Silu)
            split_hi_halves(act, 0, t + 1)
            hidden_act(act, g, t + 1, 0, True)
            split_hi(act, 1, t + 1, 4)
            step(1, 1, first=True)
            step(2, 0)
            with act.Fori(3, FFN_S - 2, 2) as s:
                step(s, 1)
                step(s + 1, 0)
            step(FFN_S - 2, 1)
            hidden_act(act, g + FFN_S - 2, t + FFN_S - 1, 1, True)
            split_hi(act, 2, t + FFN_S - 2, 4)
            ht_act(act, g + FFN_S - 2, 1, True)
            split_hi(act, 0, t + FFN_S, after[0])
            split_hi_halves(act, 2, t + FFN_S - 1)
            for i in range(TT):
                hidden_act(act, g + FFN_S - 1, t + FFN_S, 0, True, f + 1, (i,))
                ht_act(act, g + FFN_S - 1, 0, True, (i,))
            split_hi(act, 1, t + FFN_S, after[1])

        def mlp_split(split, eng, t, s, mid, after):
            split(eng, 2, t + 2 * s - 1, 2)
            mid()
            split(eng, 0, t + 2 * s, 4)
            split(eng, 1, t + 2 * s, 2)
            split(eng, 2, t + 2 * s, 2)
            split(eng, 0, t + 2 * s + 1, after[0])
            split(eng, 1, t + 2 * s + 1, after[1])

        @block.scalar
        def _(act):
            for t in range(TT):
                act.wait_ge(x_loaded[t], 16)
                rms_act(act, 0, (t,))
            split_hi(act, 0, 0, 3)
            xt_act(act, 0, toks=(0,))
            split_hi(act, 1, 0, 3)
            split_hi(act, 2, 0, 2)
            xt_act(act, 0, toks=(1,))
            for s in range(S1_SOLID):
                if s > 0:
                    read_proj1(act, s - 1)
                    split_hi(act, 2, s, 2)
                split_hi(act, 0, s + 1, 3)
                split_hi(act, 1, s + 1, 3)
                if s == 2:
                    act.wait_ge(ang_ready, 1)
                    act.activation(sinb[:, :, :], ang[:, :, :], ACT.Sin)
                    act.activation(cosb[:, :, :], part[:, :, :], ACT.Sin).then_inc(trig_ready, 1)
                    act.wait_ge(lam_sum, 1)
                    act.activation(dexp[:, :, :], dsum[:, :, :], ACT.Exp).then_inc(lam_exp, 1)
                if s in (3, 4):
                    head_square(act, s - 3)
                if s == 6:
                    head_square(act, 2)
            read_gate(act, S1_GATES)
            read_qk(act, 0, range(6), 4, QK1_TILES, 4)
            _, splits, reads = gate_plan()
            for i in range(UNITS + 2):
                if i in reads:
                    read_gate(act, reads[i])
                if i == 3:
                    head_square(act, 3)
                if i == UNITS // 2:
                    read_qk(act, 0, range(6, QK1_BANKS), 6, QK1_TILES, 2)
                if i < UNITS:
                    exps(act, True, 0, i)
                if 1 <= i <= UNITS:
                    read_pt(act, True, 0, i - 1)
                if i < UNITS:
                    for j, s, n in splits.get(i, []):
                        split_hi(act, j, s, n)
            xt_act(act, 1, 6)
            split_hi(act, 1, T_BRANCH, 4)
            split_hi(act, 2, T_BRANCH, 4)
            split_hi(act, 0, T_WOUT1, 3)
            split_hi(act, 1, T_WOUT1, 3)
            xt_act(act, 2, toks=(0,))
            split_hi(act, 2, T_WOUT1, STRIP[2])
            xt_act(act, 2, toks=(1,))
            split_hi(act, 0, T_WOUT1 + 1, 3)
            split_hi(act, 1, T_WOUT1 + 1, 3)
            split_hi(act, 2, T_WOUT1 + 1, STRIP[2])
            rms_act(act, 1, (0,))
            split_hi(act, 0, T_MLP, 3)
            split_hi(act, 1, T_MLP, 3)
            xt_act(act, 3, toks=(0,))
            split_hi(act, 2, T_MLP, STRIP[2])
            rms_act(act, 1, (1,))
            xt_act(act, 3, toks=(1,))
            def step(s, par, after=(3, 3)):
                hidden_act(act, s - 1, mlp_up(s - 1) + 1, 1 - par, False)
                mlp_split(split_hi, act, T_MLP, s, lambda: ht_act(act, s - 1, 1 - par, False), after)
            split_hi(act, 0, T_MLP + 1, 3)
            split_hi(act, 1, T_MLP + 1, 3)
            step(1, 1)
            with act.Fori(2, MLP_S - 2, 2) as s:
                step(s, 0)
                step(s + 1, 1)
            step(MLP_S - 2, 0)
            step(MLP_S - 1, 1, (4, 2))
            hidden_act(act, MLP_S - 1, mlp_up(MLP_S - 1) + 1, 1, False)
            ht_act(act, MLP_S - 1, 1, False)
            split_hi(act, 2, T_LAYER - 1, 2)
            split_hi_halves(act, 0, T_LAYER)
            xt_act(act, XT1, toks=(0,))
            split_hi(act, 1, T_LAYER, 4)
            with act.Fori(0, LAYERS) as l:
                t, g, n = T_LAYER + L_TRIPLES * l, MLP_S + 2 * FFN_S * l, XT1 * (l + 1)
                xt_act(act, n, toks=(1,))
                ffn_act(act, t, g, 2 * l, STRIP)
                xt_act(act, n + 1, toks=(0,))
                split_hi(act, 2, t + L_PROJ, STRIP[2])
                xt_act(act, n + 1, toks=(1,))
                for j in range(S2):
                    if j > 0:
                        read_proj2(act, t, j - 1)
                    if j == S2 - 1:
                        act.activation(scratch[:, :], ident[:, 0:1], ACT.Exp)
                    if j in (2, 3):
                        read_qk(act, QK1_BANKS + QK2_BANKS * l, (2 * j - 4, 2 * j - 3), 4, QK2_TILES, 3)
                    after = PROJ2[j + 1][1] if j + 1 < S2 else BW
                    if j > 0:
                        split_hi(act, 2, t + L_PROJ + j, STRIP[2], PROJ2[j][1])
                    split_hi(act, 0, t + L_PROJ + j + 1, 3, after)
                    split_hi(act, 1, t + L_PROJ + j + 1, 3, after)
                read_qk(act, QK1_BANKS + QK2_BANKS * l, (4, 5, 6), 4, QK2_TILES, 3)
                read_proj2(act, t, S2 - 1)
                for i in range(UNITS + 2):
                    if i >= 2:
                        read_pt(act, False, UNITS * (l + 1), i - 2)
                    if 1 <= i <= UNITS:
                        exps(act, False, UNITS * (l + 1), i - 1)
                    if i == 4:
                        split_hi(act, 2, t + L_WOUT, 2)
                xt_act(act, n + 2)
                split_hi(act, 0, t + L_WOUT + 1, 3)
                split_hi(act, 1, t + L_WOUT + 1, 3)
                split_hi(act, 2, t + L_WOUT + 1, STRIP[2])
                split_hi(act, 0, t + L_FFN2, 4)
                split_hi(act, 1, t + L_FFN2, 4)
                xt_act(act, n + 3)
                ffn_act(act, t + L_FFN2, g + FFN_S, 2 * l + 1, (4, 4))
                xt_act(act, n + 4, toks=(0,))

        def xt_dve(dve, n, tiles=KD, toks=range(TT)):
            for t in toks:
                for b in range(2):
                    m = min(4, tiles - 4 * b)
                    ks, tok = slice(4 * b, 4 * b + m), slice(t * P, (t + 1) * P)
                    dve.wait_ge(xt_hi_done, 4 * n + 2 * t + b + 1)
                    dve.tensor_tensor(xt_lo[:, ks, tok], ps[:, 2 * t + b, 0:m * P].rearrange("p (k n) -> p k n", k=m),
                                      xt_hi[:, ks, tok].bitcast(F32), ALU.subtract).then_inc(xt_lo_done, 1)

        def maxima(dve, first, base, u):
            if u >= 3:
                dve.wait_ge(pt_ready, base + u - 2)
            dve.wait_ge(s_ready, base + u + 1)
            i = u % 4
            e, s = ebuf[u % 3], set_of(first, u)
            g = (u - UNITS // 2) // TT
            if u >= UNITS // 2:
                dve.tensor_scalar(nsink[:, i, :], (sink1 if first else sinkc)[:, g:8:4], -1.0, None, ALU.mult)
            if u < UNITS // 2:
                if first:
                    w = width_of(first, u)
                    n = w // DIL_G
                    dve.tensor_tensor_reduce(e[:, 0:w].rearrange("p (g n) -> p g n", g=DIL_G),
                                             s[:, 0:w].rearrange("p (g n) -> p g n", g=DIL_G),
                                             mask[:, 0:DIL_G, TOK - n:TOK], SCALE, -3e38, ALU.add, ALU.max, top[:, i, 0:1])
                    dve.drain()
                    dve.tensor_scalar(ntop[:, i, 0:1], top[:, i, 0:1], -1.0, None, ALU.mult).then_inc(top_ready, 1)
                    return
                dve.tensor_reduce(top[:, i, :], s.rearrange("p (r n) -> p r n", r=2)[:, :, 0:TOK], AX.X, ALU.max)
                dve.drain()
                dve.tensor_scalar(ntop[:, i, :], top[:, i, :], -SCALE, None, ALU.mult).then_inc(top_ready, 1)
                return
            w = width_of(first, u) // KV
            kind = 3 if first else 4 + u % TT
            for r in range(KV):
                dve.tensor_tensor_reduce(e[:, r * w:(r + 1) * w], s[:, r * BW:r * BW + w], mask[:, kind, TOK - w:TOK],
                                         SCALE, -3e38, ALU.add, ALU.max, top[:, i, r:r + 1])
            dve.drain()
            dve.scalar_tensor_tensor(ntop[:, i, :], top[:, i, :], -1.0, nsink[:, i, :],
                                     ALU.mult, ALU.min).then_inc(top_ready, 1)

        def reciprocals(dve, first, base, pairs, u):
            if u < UNITS // 2:
                dve.wait_ge(e_ready, base + u + 1)
            else:
                dve.wait_ge(esink_ready, pairs + u - UNITS // 2 + 1)
            i = u % 4
            if first and u < UNITS // 2:
                dve.reciprocal(rden[:, i, 0:1], den[:, i, 0:1])
                return
            if u >= UNITS // 2:
                dve.tensor_tensor(den[:, i, :], den[:, i, :], esink[:, i, :], ALU.add)
                dve.drain()
                dve.reciprocal(rden[:, i, :], den[:, i, :])
                return
            dve.reciprocal(rden[:, i, :], den[:, i, :])
            dve.drain()
            dve.tensor_tensor(rden[:, i, 1:2], rden[:, i, 1:2], lamc[:, :], ALU.mult)

        def read_out(dve, first, base, u):
            dve.wait_ge(o_ready, base + u + 1)
            o, qt = ps[:, 6 + u % 2, :], u % TT
            if not first and u < UNITS // 2:
                h = u // TT
                dve.tensor_scalar(second[:, :], o[:, 2 * HD:4 * HD], rden[:, u % 4, 1:2], None, ALU.mult)
                dve.drain()
                dve.scalar_tensor_tensor(heads_out[:, qt, h * 2 * HD:(h + 1) * 2 * HD], o[:, 0:2 * HD],
                                         rden[:, u % 4, 0:1], second[:, :], ALU.mult, ALU.subtract).then_inc(o_out, 1)
                return
            if u < UNITS // 2:
                cols = [u // TT * HD]
            else:
                g = (u - UNITS // 2) // TT
                cols = [(OA_W if first else BW) + (4 * r + g) * HD for r in range(KV)]
            for r, c in enumerate(cols):
                m = dve.tensor_scalar(heads_out[:, qt, c:c + HD], o[:, r * HD:(r + 1) * HD],
                                      rden[:, u % 4, r:r + 1], None, ALU.mult)
            m.then_inc(o_out, 1)

        def sum_squares(dve, i):
            heads = NORMS[i][0]
            dve.wait_ge(head_sq, i + 1)
            dve.tensor_reduce(ssum[:, 0:heads], square[:, 0:heads * HD].rearrange("p (h d) -> p h d", d=HD),
                              AX.X, ALU.add).then_inc(head_ss, 1)

        def norm_heads(dve, i):
            heads, col = NORMS[i]
            t = i % 2
            v = proj[:, t, col:col + heads * HD].rearrange("p (h d) -> p h d", d=HD)
            dve.wait_ge(head_rstd, i + 1)
            dve.tensor_tensor(v, v, rstd[:, 0:heads].unsqueeze(2).to_broadcast([P, heads, HD]), ALU.mult)
            dve.drain()
            if i < 2:
                g = v.rearrange("p (g h) d -> p g h d", g=2)
                dve.tensor_tensor(g, g, gain[:, 0:2, :].unsqueeze(2).to_broadcast([P, 2, 12, HD]), ALU.mult)
            else:
                dve.tensor_tensor(v[:, 0:8, :], v[:, 0:8, :], gain[:, 2:3, :].to_broadcast([P, 8, HD]), ALU.mult)
                dve.tensor_tensor(v[:, 8:10, :], v[:, 8:10, :], gain[:, 3:4, :].to_broadcast([P, 2, HD]), ALU.mult)
            dve.drain()
            if i == 0:
                dve.wait_ge(trig_ready, 1)
            tmp = [rope[:, j, 0:heads * ROPE1].rearrange("p (h d) -> p h d", d=ROPE1) for j in range(4)]
            c, s = (z[:, t:t + 1, 0:ROPE1].to_broadcast([P, heads, ROPE1]) for z in (cosb, sinb))
            rotate(dve, v[:, :, 0:ROPE1], v[:, :, ROPE1:2 * ROPE1], c, s, *tmp).then_inc(roped, 1)

        def rms_dve(dve, i, toks=range(TT)):
            dve.wait_ge(g_loaded, 16 * (i + 1))
            for t in toks:
                dve.wait_ge(rms_rstd, 2 * i + t + 1)
                dve.scalar_tensor_tensor(normed[:, t, :], xres[:, t, :], lrs[:, t:t + 1], ln_g[:, :],
                                         ALU.mult, ALU.mult).then_inc(xt_src, 2)

        def hidden_dve(dve, g, par, ffn, toks=range(TT)):
            w = FFN_H if ffn else BW
            for t in toks:
                dve.wait_ge(hid_act, 2 * g + t + 1)
                other = ps[:, 2 * par + t, w:2 * w] if ffn else hid_a[:, t, 0:w]
                dve.tensor_tensor(hid_b[:, t, 0:w], hid_a[:, t, 0:w], other, ALU.mult).then_inc(hid_ready, 1)

        def ht_dve(dve, g, par, ffn, toks=range(TT)):
            k = (FFN_H if ffn else BW) // P
            for t in toks:
                tok = slice(t * P, (t + 1) * P)
                dve.wait_ge(ht_hi_done, 2 * g + t + 1)
                dve.tensor_tensor(ht_lo[:, 0:k, tok], ps[:, 2 * par + t, 0:k * P].rearrange("p (k n) -> p k n", k=k),
                                  ht_hi[:, 0:k, tok].bitcast(F32), ALU.subtract).then_inc(ht_lo_done, 1)

        def ffn_dve(dve, t, g, f, after0):
            def step(s, par, n=(4, 4), first=False):
                if not first:
                    hidden_dve(dve, g + s - 1, 1 - par, True)
                split_lo(dve, 2, t + s - 1, 4)
                ht_dve(dve, g + s - 1, 1 - par, True)
                split_lo(dve, 0, t + s + 1, n[0])
                split_lo(dve, 1, t + s + 1, n[1])
            split_lo_halves(dve, 0, t + 1, 2 * f + 2)
            hidden_dve(dve, g, 0, True)
            split_lo(dve, 1, t + 1, 4)
            step(1, 1, first=True)
            step(2, 0)
            with dve.Fori(3, FFN_S - 2, 2) as s:
                step(s, 1)
                step(s + 1, 0)
            step(FFN_S - 2, 1)
            hidden_dve(dve, g + FFN_S - 2, 1, True)
            split_lo(dve, 2, t + FFN_S - 2, 4)
            ht_dve(dve, g + FFN_S - 2, 1, True)
            split_lo(dve, 0, t + FFN_S, after0)
            split_lo_halves(dve, 2, t + FFN_S - 1, 2 * f + 3)
            for i in range(TT):
                hidden_dve(dve, g + FFN_S - 1, 0, True, (i,))
                ht_dve(dve, g + FFN_S - 1, 0, True, (i,))

        def split_first(dve, t):
            dve.wait_ge(hi_done[0], t + 1)
            dve.tensor_tensor(wlo[0][:, 0:2, :], raw[0][:, 0:2, :], whi[0][:, 0:2, :].bitcast(F32),
                              ALU.subtract).then_inc(lo_first, 1)

        def norm_dve(dve, q, n, done, ffn, parts, split=None, rest=True):
            def add(t, h):
                xs, y = xres[:, t, h * BW:(h + 1) * BW], ps[:, (4 + 2 * t + h) if ffn else (2 * h + t), :]
                if ffn and (t, h) != (1, 1):
                    dve.wait_ge(y_part, parts + 2 * t + h + 1)
                elif t == 0:
                    dve.wait_ge(y_part, parts + 1)
                else:
                    dve.wait_ge(used[2], done)
                dve.scalar_tensor_tensor(xs, y, (0.5 if ffn else 1.0) / ALPHA, xs, ALU.mult, ALU.add)

            def stat(t, h):
                dve.drain()
                dve.bn_stats(stats[:, t, h, :], xres[:, t, h * BW:(h + 1) * BW])

            def centre(t):
                dve.drain()
                dve.bn_aggr(mv[:, t, :], stats[:, t, :, :].rearrange("p h n -> p (h n)")).then_inc(var_ready, 1)
                dve.drain()
                if t == 0:
                    dve.wait_ge(g_loaded, 32 * (q + 2))
                dve.scalar_tensor_tensor(xres[:, t, :], xres[:, t, :], mv[:, t, 0:1], ln_g[:, :], ALU.subtract, ALU.mult)

            def scale(t):
                dve.drain()
                dve.wait_ge(lrs_ready, 2 * q + t + 1)
                for h in range(2):
                    cols = slice(h * BW, (h + 1) * BW)
                    dve.scalar_tensor_tensor(xres[:, t, cols], xres[:, t, cols], lrs[:, t:t + 1], ln_b[:, cols],
                                             ALU.mult, ALU.add).then_inc(xt_src, 1)
            halves = range(2) if ffn else (1,)
            for h in range(2):
                if h in halves:
                    add(0, h)
                stat(0, h)
            centre(0)
            scale(0)
            if ffn:
                add(1, 0)
            if split is not None:
                split()
            if not ffn:
                add(1, 1)
            xt_dve(dve, n, toks=(0,))
            if ffn:
                add(1, 1)
            for h in range(2):
                stat(1, h)
            centre(1)
            scale(1)
            if rest:
                xt_dve(dve, n, toks=(1,))

        def angles(dve):
            dve.wait_ge(consts_set, 1)
            dve.wait_ge(const_loaded, 16 * 10)
            dve.tensor_copy(pos_f[:, :, :], pos_i[:, :, :])
            dve.drain()
            for t in range(TT):
                for b, (a, z) in enumerate(((0, ROPE1), (ROPE1, ROPES))):
                    dve.tensor_scalar(ang[:, t, a:z], inv[:, a:z], pos_f[:, b, t:t + 1], None, ALU.mult)
            dve.drain()
            dve.tensor_scalar(turns[:, :, :], ang[:, :, :], 1.0 / (2 * math.pi), ROUND, ALU.mult, ALU.add)
            dve.drain()
            dve.tensor_scalar(turns[:, :, :], turns[:, :, :], ROUND, None, ALU.subtract)
            for c in TWO_PI:
                dve.drain()
                dve.scalar_tensor_tensor(ang[:, :, :], turns[:, :, :], -c, ang[:, :, :], ALU.mult, ALU.add)
            dve.drain()
            dve.tensor_scalar(ang[:, :, :], ang[:, :, :], PI_LOW, -PI_LOW, ALU.min, ALU.max)
            dve.drain()
            dve.scalar_tensor_tensor(part[:, :, :], ang[:, :, :], -1.0, ang[:, :, :], ALU.mult, ALU.min)
            dve.drain()
            dve.tensor_scalar(part[:, :, :], part[:, :, :], math.pi / 2, None, ALU.add).then_inc(ang_ready, 1)

        def stride_masks(dve):
            for b, bits in enumerate((3, 15)):
                dve.tensor_scalar(dist4[:, b, :], dist[:, :], bits, None, ALU.bitwise_and)
            dve.drain()
            for b in range(2):
                for j in range(2):
                    m = dve.tensor_scalar(mask[:, 1 + b, j * P:(j + 1) * P], dist4[:, b, :], 0.0, NEG,
                                          ALU.not_equal, ALU.mult)
            m.then_inc(mask_mod, 1)

        def lambdas_sums(dve):
            dve.tensor_tensor(dprod[:, :, :, :], dlam[:, :, 0:4:2, :], dlam[:, :, 1:4:2, :], ALU.mult)
            dve.drain()
            dve.tensor_reduce(dsum[:, :, :], dprod[:, :, :, :], AX.X, ALU.add).then_inc(lam_sum, 1)

        def lambdas(dve):
            dve.wait_ge(lam_exp, 1)
            for l, init in enumerate(LAMBDA_INIT):
                dve.scalar_tensor_tensor(lam[:, l:l + 1], dexp[:, l, 0:1], init, dexp[:, l, 1:2], ALU.add, ALU.subtract)
                dve.tensor_scalar(subg[:, l, :], subg[:, l, :], 1.0 - init, None, ALU.mult)

        @block.vector
        def _(dve):
            rms_dve(dve, 0)
            split_lo(dve, 0, 0, 3)
            xt_dve(dve, 0, toks=(0,))
            split_lo(dve, 1, 0, 3)
            split_lo(dve, 2, 0, 2)
            xt_dve(dve, 0, toks=(1,))
            for s in range(S1_SOLID):
                if s > 0:
                    split_lo(dve, 2, s, 2)
                split_lo(dve, 0, s + 1, 3)
                split_lo(dve, 1, s + 1, 3)
                if s == 0:
                    angles(dve)
                    stride_masks(dve)
                    lambdas_sums(dve)
                if s == 3:
                    lambdas(dve)
                    sum_squares(dve, 0)
                if s == 4:
                    norm_heads(dve, 0)
                    sum_squares(dve, 1)
                if s == 5:
                    norm_heads(dve, 1)
            sum_squares(dve, 2)
            norm_heads(dve, 2)
            _, splits, _ = gate_plan()
            dve.wait_ge(mask_pool, 1)
            for i in range(UNITS + 2):
                if i < UNITS:
                    maxima(dve, True, 0, i)
                if 1 <= i <= UNITS:
                    reciprocals(dve, True, 0, 0, i - 1)
                if i >= 2:
                    if i == UNITS + 1:
                        dve.drain()
                    read_out(dve, True, 0, i - 2)
                if i == 3:
                    sum_squares(dve, 3)
                if i == 5:
                    norm_heads(dve, 3)
                if i < UNITS:
                    for j, s, n in splits.get(i, []):
                        split_lo(dve, j, s, n)
            dve.drain().then_inc(xt_src, 4)
            xt_dve(dve, 1, 6)
            split_lo(dve, 1, T_BRANCH, 4)
            split_lo(dve, 2, T_BRANCH, 4)
            dve.wait_ge(gate_half, S1 - S1_GATES)
            dve.wait_ge(used[0], T_BRANCH + 1)
            for t in range(TT):
                dve.tensor_tensor(mixed[:, t, :], ps[:, 2 * t:2 * t + 2, :].rearrange("p b n -> p (b n)"),
                                  gates[:, t, 0:DM], ALU.mult)
            split_lo(dve, 0, T_WOUT1, 3)
            for t in range(TT):
                if t == 0:
                    dve.wait_ge(branch_tile0, 1)
                else:
                    split_lo(dve, 1, T_WOUT1, 3)
                    xt_dve(dve, 2, toks=(0,))
                    dve.wait_ge(used[2], T_BRANCH + 1)
                dve.tensor_tensor(mix_b[:, t, :], ps[:, 4 + 2 * t:6 + 2 * t, :].rearrange("p b n -> p (b n)"),
                                  gates[:, t, DM:2 * DM], ALU.mult)
                dve.drain()
                dve.tensor_tensor(mixed[:, t, :], mixed[:, t, :], mix_b[:, t, :], ALU.add).then_inc(xt_src, 2)
            split_lo(dve, 2, T_WOUT1, STRIP[2])
            xt_dve(dve, 2, toks=(1,))
            split_lo(dve, 0, T_WOUT1 + 1, 3)
            split_lo(dve, 1, T_WOUT1 + 1, 3)
            dve.wait_ge(used[2], T_WOUT1 + 1)
            for t in range(TT):
                dve.tensor_tensor(xres[:, t, 0:BW], xres[:, t, 0:BW], ps[:, t, :], ALU.add)
            split_lo(dve, 2, T_WOUT1 + 1, STRIP[2])
            dve.wait_ge(y_part, 1)
            dve.tensor_tensor(xres[:, 0, BW:DM], xres[:, 0, BW:DM], ps[:, 2, :], ALU.add).then_inc(res_ready, 1)
            rms_dve(dve, 1, (0,))
            split_lo(dve, 0, T_MLP, 3)
            xt_dve(dve, 3, toks=(0,))
            dve.wait_ge(used[2], T_WOUT1 + 2)
            dve.tensor_tensor(xres[:, 1, BW:DM], xres[:, 1, BW:DM], ps[:, 3, :], ALU.add).then_inc(res_ready, 1)
            split_lo(dve, 2, T_MLP, STRIP[2])
            rms_dve(dve, 1, (1,))
            xt_dve(dve, 3, toks=(1,))
            def step(s, par, after=(3, 3)):
                hidden_dve(dve, s - 1, 1 - par, False)
                mlp_split(split_lo, dve, T_MLP, s, lambda: ht_dve(dve, s - 1, 1 - par, False), after)
            split_lo(dve, 0, T_MLP + 1, 3)
            split_lo(dve, 1, T_MLP + 1, 3)
            step(1, 1)
            with dve.Fori(2, MLP_S - 2, 2) as s:
                step(s, 0)
                step(s + 1, 1)
            step(MLP_S - 2, 0)
            step(MLP_S - 1, 1, (4, 2))
            hidden_dve(dve, MLP_S - 1, 1, False)
            ht_dve(dve, MLP_S - 1, 1, False)
            split_lo(dve, 2, T_LAYER - 1, 2)
            for t in range(TT):
                if t == 0:
                    dve.wait_ge(y_part, 2)
                else:
                    split_lo_halves(dve, 0, T_LAYER, 1)
                    xt_dve(dve, XT1, toks=(0,))
                    dve.wait_ge(used[2], T_LAYER)
                dve.tensor_tensor(xres[:, t, :], xres[:, t, :], ps[:, 4 + 2 * t:6 + 2 * t, :].rearrange("p b n -> p (b n)"),
                                  ALU.add).then_inc(xt_src, 2)
            split_lo(dve, 1, T_LAYER, 4)
            with dve.Fori(0, LAYERS) as l:
                t, g, n, q = T_LAYER + L_TRIPLES * l, MLP_S + 2 * FFN_S * l, XT1 * (l + 1), 3 * l
                base = UNITS * (l + 1)
                xt_dve(dve, n, toks=(1,))
                dve.tensor_copy(lamc[:, :], lam[:, ds(l, 1)])
                dve.tensor_copy(sinkc[:, :], sink2[:, ds(l, 1), :])
                dve.tensor_copy(subgc[:, :], subg[:, ds(l, 1), :])
                ffn_dve(dve, t, g, 2 * l, STRIP[0])
                norm_dve(dve, q, n + 1, t + FFN_S, True, 2 + Y_PARTS * l)
                for j in range(S2):
                    if j > 0:
                        rotate_strip(dve, l, j - 1, 0, rope, roped)
                    after = PROJ2[j + 1][1] if j + 1 < S2 else BW
                    if j > 0:
                        split_lo(dve, 2, t + L_PROJ + j, STRIP[2], PROJ2[j][1])
                    split_lo(dve, 0, t + L_PROJ + j + 1, 3, after)
                    split_lo(dve, 1, t + L_PROJ + j + 1, 3, after)
                for i in range(UNITS + 2):
                    if i >= 2:
                        reciprocals(dve, False, base, UNITS // 2 * (l + 1), i - 2)
                    if i < UNITS:
                        maxima(dve, False, base, i)
                    else:
                        dve.drain()
                    if i >= 2:
                        read_out(dve, False, base, i - 2)
                    if i == UNITS // 2 + 3:
                        dve.wait_ge(dsq, l + 1)
                        dve.tensor_reduce(dss[:, :].rearrange("p (t h) -> p t h", t=TT),
                                          square[:, 0:TT * BW].rearrange("p (t h d) -> p t h d", t=TT, d=2 * HD),
                                          AX.X, ALU.add).then_inc(dsum_ready, 1)
                dve.wait_ge(heads_normed, l + 1)
                dve.drain().then_inc(xt_src, 4)
                xt_dve(dve, n + 2)
                split_lo(dve, 0, t + L_WOUT + 1, 3)
                split_lo(dve, 1, t + L_WOUT + 1, 3)
                dve.wait_ge(used[2], t + L_WOUT + 1)
                for k in range(TT):
                    xs = xres[:, k, 0:BW]
                    dve.scalar_tensor_tensor(xs, ps[:, k, :], 1.0 / ALPHA, xs, ALU.mult, ALU.add)
                split_lo(dve, 2, t + L_WOUT + 1, STRIP[2])
                norm_dve(dve, q + 1, n + 3, t + L_WOUT + 2, False, 5 + Y_PARTS * l,
                         split=lambda: split_first(dve, t + L_FFN2))
                ffn_dve(dve, t + L_FFN2, g + FFN_S, 2 * l + 1, 4)
                norm_dve(dve, q + 2, n + 4, t + L_TRIPLES, True, 6 + Y_PARTS * l, rest=False)

        def block_mm(pe, hi, lo, k, slot, b, banks, start, stop, width=BW):
            for t in range(TT):
                o, tok = ps[:, banks[t], 0:width], slice(t * P, (t + 1) * P)
                pe.matmul(o, hi[:, k, tok], whi[slot][:, b, 0:width], start=start, stop=False)
                pe.matmul(o, hi[:, k, tok], wlo[slot][:, b, 0:width], start=False, stop=False)
                m = pe.matmul(o, lo[:, k, tok], whi[slot][:, b, 0:width], start=False, stop=stop)
            return m

        def tile_mm(pe, hi, lo, k, slot, b, t, bank, start, stop, width=BW):
            o, tok = ps[:, bank, 0:width], slice(t * P, (t + 1) * P)
            pe.matmul(o, hi[:, k, tok], whi[slot][:, b, 0:width], start=start, stop=False)
            pe.matmul(o, hi[:, k, tok], wlo[slot][:, b, 0:width], start=False, stop=False)
            return pe.matmul(o, lo[:, k, tok], whi[slot][:, b, 0:width], start=False, stop=stop)

        def strip_block(pe, t, k, banks, width=BW):
            slot = 0 if k < 3 else 1 if k < 6 else 2
            b = k - sum(STRIP[:slot])
            if b == 0:
                pe.wait_ge(lo_done[slot], t + 1)
            m = block_mm(pe, xt_hi, xt_lo, k, slot, b, banks, k == 0, k == KD - 1, width)
            if b == STRIP[slot] - 1:
                m.then_inc(used[slot], 1)

        def strip(pe, t, banks, width=BW, between=None, at=2):
            for k in range(KD):
                strip_block(pe, t, k, banks, width)
                if between is not None and k == at:
                    between()

        def pair(par):
            return (2 * par, 2 * par + 1)

        def xt_tile_pe(pe, n, t, src, tiles=KD):
            for b in range(2):
                pe.wait_ge(xt_src, 4 * n + 2 * t + b + 1)
                for i, k in enumerate(range(4 * b, min(4 * b + 4, tiles))):
                    m = pe.transpose(ps[:, 2 * t + b, i * P:(i + 1) * P], src[:, t, k * P:(k + 1) * P], ident[:, :])
                m.then_inc(xt_tr, 1)

        def first_strip(pe, n, src, T, chunks, width=BW, at=2, turned=False, mix=None):
            seq = [(slot, b) for slot, blocks in enumerate(chunks) for b in range(blocks)]
            if not turned:
                xt_tile_pe(pe, n, 0, src)
            for t in range(TT):
                for k, (slot, b) in enumerate(seq):
                    if k % 4 == 0:
                        pe.wait_ge(xt_lo_done, 4 * n + 2 * t + k // 4 + 1)
                    if t == 0 and k == 0 and mix is not None:
                        pe.wait_ge(lo_first, mix + 1)
                    elif t == 0 and (b == 0 or k == 2 and mix is not None):
                        pe.wait_ge(lo_done[slot], T + 1)
                    m = tile_mm(pe, xt_hi, xt_lo, k, slot, b, t, t, k == 0, k == KD - 1, width)
                    if t == 1 and b == chunks[slot] - 1:
                        m.then_inc(used[slot], 1)
                    if t == 0 and k == at:
                        xt_tile_pe(pe, n, 1, src)

        def last_strip(pe, T, bank0, late=None):
            for t in range(TT):
                for k in range(KD):
                    slot = 0 if k < 3 else 1 if k < 6 else 2
                    b = k - sum(STRIP[:slot])
                    if t == 0 and b == 0:
                        pe.wait_ge(lo_done[slot], T + 1)
                    if t == 1 and k == 6 and late is not None:
                        late()
                    m = tile_mm(pe, xt_hi, xt_lo, k, slot, b, t, bank0 + t, k == 0, k == KD - 1)
                    if t == 1 and b == STRIP[slot] - 1:
                        m.then_inc(used[slot], 1)
                if t == 0:
                    m.then_inc(y_part, 1)

        def qk_pe(pe, base, events, bank0, banks, src, tiles):
            for e in events:
                if e >= banks:
                    pe.wait_ge(qk_out, base + e - banks + 1)
                for i in range(min(2, tiles - 2 * e)):
                    for t in range(TT):
                        m = pe.transpose(ps[:, bank0 + e % banks, (2 * i + t) * P:(2 * i + t + 1) * P],
                                         src(2 * e + i, t), ident[:, :])
                m.then_inc(qk_tr, 1)

        def qk_src1(tile, t):
            c = tile * P if tile < 12 else QB1 + (tile - 12) * P
            return proj[:, t, c:c + P]

        def qk_src2(tile, t):
            c = tile * P if tile < 8 else SQ2 + (tile - 8) * P
            return proj[:, t, c:c + P]

        def scores(pe, first, base, u):
            ns = 2 if first else 3
            if u >= ns:
                pe.wait_ge(pt_out, base + u - ns + 1)
            s, qt = set_of(first, u), u % TT
            n = P * (qt + 1) if first else TOK
            if u < UNITS // 2:
                h = u // TT
                if first:
                    parts = [(h % 2, 2 * g + h // 2, 6 + 2 * g + h // 2) for g in range(DIL_G)]
                else:
                    parts = [(c, h, 4 + h) for c in range(2)]
            else:
                g = (u - UNITS // 2) // TT
                parts = [(r, (12 if first else 8) + g, 16 if first else 12) for r in range(KV)]
            for i, (r, qtile, ktile) in enumerate(parts):
                rows = slice(r * HD, (r + 1) * HD)
                c = i * (n if len(parts) == DIL_G else BW)
                m = pe.matmul(s[:, c:c + n], qkt[rows, qtile, qt * P:(qt + 1) * P], qkt[rows, ktile, 0:n],
                              start=True, stop=True)
            m.then_inc(s_ready, 1)

        def turn_probs(pe, first, base, u):
            pe.wait_ge(e_ready, base + u + 1)
            s = set_of(first, u)
            for j in range(width_of(first, u) // P):
                m = pe.transpose(s[:, j * P:(j + 1) * P], ebuf[u % 3][:, j * P:(j + 1) * P], ident[:, :])
            m.then_inc(pt_ready, 1)

        def outputs(pe, first, base, u):
            pe.wait_ge(pt_out, base + u + 1)
            if u >= 2:
                pe.wait_ge(o_out, base + u - 1)
            o, pt, qt = ps[:, 6 + u % 2, :], ptb[u % 2], u % TT
            nk = qt + 1 if first else TT
            if u < UNITS // 2:
                h = u // TT
                if first:
                    rows = [(o[:, 0:HD], [(g * nk + k, proj[:, k, V1 + (4 * g + h) * HD:V1 + (4 * g + h + 1) * HD])
                                          for g in range(DIL_G) for k in range(nk)])]
                else:
                    rows = [(o[:, r * 2 * HD:(r + 1) * 2 * HD],
                             [(r * nk + k, proj[:, k, DV2 + h * 2 * HD:DV2 + (h + 1) * 2 * HD]) for k in range(nk)])
                            for r in range(2)]
            else:
                v = VB1 if first else SV2
                rows = [(o[:, r * HD:(r + 1) * HD],
                         [(r * nk + k, proj[:, k, v + r * HD:v + (r + 1) * HD]) for k in range(nk)]) for r in range(KV)]
            for dst, terms in rows:
                for i, (j, v) in enumerate(terms):
                    m = pe.matmul(dst, pt[:, j * P:(j + 1) * P], v, start=i == 0, stop=i == len(terms) - 1)
            m.then_inc(o_ready, 1)

        def hid_tile_pe(pe, g, par, t, ffn):
            pe.wait_ge(hid_ready, 2 * g + t + 1)
            for k in range((FFN_H if ffn else BW) // P):
                m = pe.transpose(ps[:, 2 * par + t, k * P:(k + 1) * P], hid_b[:, t, k * P:(k + 1) * P], ident[:, :])
            m.then_inc(hid_tr, 1)

        def hid_tr_pe(pe, g, par, ffn):
            for t in range(TT):
                hid_tile_pe(pe, g, par, t, ffn)

        def ffn_in_chunk(pe, t, par, slot, between=None, part=None):
            if part is None:
                pe.wait_ge(lo_done[slot], t + 1)
            for b in range(4):
                if part is not None and b == 0:
                    pe.wait_ge(lo_half, part)
                if part is not None and b == 2:
                    pe.wait_ge(lo_done[slot], t + 1)
                k = 4 * slot + b
                m = block_mm(pe, xt_hi, xt_lo, k, slot, b, pair(par), k == 0, k == KD - 1)
                if b == 3:
                    m.then_inc(used[slot], 1)
                if b == 1 and between is not None:
                    between()

        def last_in_chunk(pe, t, par, g):
            pe.wait_ge(lo_done[1], t + 1)
            for i in range(TT):
                for b in range(4):
                    m = tile_mm(pe, xt_hi, xt_lo, 4 + b, 1, b, i, 2 * par + i, False, b == 3)
                    if i == 1 and b == 2:
                        hid_tile_pe(pe, g, par, 0, True)
                m.then_inc(in_tile0 if i == 0 else used[1], 1)

        def down(pe, t, slots, g, first, last):
            pe.wait_ge(ht_lo_done, 2 * g + 2)
            for slot, ks in slots:
                pe.wait_ge(lo_done[slot], t + 1)
                for i, k in enumerate(ks):
                    for h in range(2):
                        m = block_mm(pe, ht_hi, ht_lo, k, slot, 2 * i + h, (4 + h, 6 + h), first and k == 0,
                                     last and slot == slots[-1][0] and k == slots[-1][1][-1])
                m.then_inc(used[slot], 1)

        def last_down_ffn(pe, t, g):
            for i in range(TT):
                pe.wait_ge(ht_lo_done, 2 * g + i + 1)
                if i == 0:
                    pe.wait_ge(lo_done[2], t + 1)
                for h in range(2):
                    for k in range(2):
                        m = tile_mm(pe, ht_hi, ht_lo, k, 2, 2 * k + h, i, 4 + 2 * i + h, False, k == 1)
                        if i == 0 and h == 0 and k == 0:
                            hid_tile_pe(pe, g, 0, 1, True)
                    if i == 1 and h == 1:
                        m.then_inc(used[2], 1)
                    else:
                        m.then_inc(y_part, 1)

        def last_down(pe, t, slots, g, par, ffn):
            hid_tile_pe(pe, g, par, 0, ffn)
            for i in range(TT):
                pe.wait_ge(ht_lo_done, 2 * g + i + 1)
                for slot, ks in slots:
                    if i == 0:
                        pe.wait_ge(lo_done[slot], t + 1)
                    elif slot == slots[-1][0]:
                        xt_tile_pe(pe, XT1, 0, xres)
                    for j, k in enumerate(ks):
                        for h in range(2):
                            m = tile_mm(pe, ht_hi, ht_lo, k, slot, 2 * j + h, i, 4 + 2 * i + h, False, k == slots[-1][1][-1])
                        if i == 0 and j == 0 and slot == slots[0][0]:
                            hid_tile_pe(pe, g, par, 1, ffn)
                    if i == 1:
                        m.then_inc(used[slot], 1)
                if i == 0:
                    m.then_inc(y_part, 1)

        FFN_DOWN = ((2, (0, 1)),)
        MLP_DOWN = ((0, (0, 1)), (1, (2,)), (2, (3,)))

        def ffn_pe(pe, t, g, f, n, turned, mix=None):
            def step(s, par, first=False):
                turn = lambda: hid_tr_pe(pe, g + s - 1, 1 - par, True)
                ffn_in_chunk(pe, t + s, par, 0, None if first else turn, 2 * f + 2 if first else None)
                ffn_in_chunk(pe, t + s, par, 1, turn if first else None)
                down(pe, t + s - 1, FFN_DOWN, g + s - 1, first, False)
            first_strip(pe, n, xres, t, (4, 4), at=5, turned=turned, mix=mix)
            step(1, 1, True)
            step(2, 0)
            with pe.Fori(3, FFN_S - 2, 2) as s:
                step(s, 1)
                step(s + 1, 0)
            step(FFN_S - 2, 1)
            ffn_in_chunk(pe, t + FFN_S - 1, 0, 0, lambda: hid_tr_pe(pe, g + FFN_S - 2, 1, True))
            down(pe, t + FFN_S - 2, FFN_DOWN, g + FFN_S - 2, False, False)
            last_in_chunk(pe, t + FFN_S - 1, 0, g + FFN_S - 1)
            last_down_ffn(pe, t + FFN_S - 1, g + FFN_S - 1)

        @block.tensor
        def _(pe):
            pe.wait_ge(ident_ready, 1)
            first_strip(pe, 0, normed, 0, STRIP)
            strip(pe, 1, pair(1))
            with pe.Fori(2, S1_GATES, 2) as s:
                for par in range(2):
                    pe.wait_ge(proj_out, 2 * (s + par) - 2)
                    strip(pe, s + par, pair(par))
            pe.wait_ge(proj_out, 2 * (S1_GATES - 1))
            strip(pe, S1_GATES, pair(0))
            pe.wait_ge(roped, 2)
            qk_pe(pe, 0, range(6), 4, 4, qk_src1, QK1_TILES)
            blocks, _, _ = gate_plan()
            pe.wait_ge(proj_out, 2 * S1_GATES)
            for i in range(UNITS + 2):
                if i == 0:
                    pe.wait_ge(qk_out, 6)
                if i == UNITS // 2:
                    pe.wait_ge(roped, 4)
                    pe.wait_ge(o_out, i - 2)
                    qk_pe(pe, 0, range(6, QK1_BANKS), 6, 2, qk_src1, QK1_TILES)
                    pe.wait_ge(qk_out, QK1_BANKS)
                if i < UNITS:
                    scores(pe, True, 0, i)
                if 1 <= i <= UNITS:
                    turn_probs(pe, True, 0, i - 1)
                if i >= 2:
                    outputs(pe, True, 0, i - 2)
                for b in blocks[i]:
                    s = S1_SOLID + b // KD
                    if b % KD == 0:
                        pe.wait_ge(proj_out, 2 * s)
                    strip_block(pe, s, b % KD, pair(0))
            pe.wait_ge(proj_out, 2 * S1)
            for t in range(TT):
                xt_tile_pe(pe, 1, t, heads_out, 6)
            pe.wait_ge(lo_done[0], T_BRANCH + 1)
            for t in range(TT):
                for h in range(2):
                    pe.wait_ge(xt_lo_done, 4 + 2 * t + h + 1)
                    for k in range(2):
                        m = tile_mm(pe, xt_hi, xt_lo, k, 0, 2 * k + h, t, 2 * t + h, k == 0, k == 1)
            m.then_inc(used[0], 1)
            for t in range(TT):
                for slot in (1, 2):
                    if t == 0:
                        pe.wait_ge(lo_done[slot], T_BRANCH + 1)
                    for k in range(2):
                        for h in range(2):
                            m = tile_mm(pe, xt_hi, xt_lo, 2 * slot + k, slot, 2 * k + h, t, 4 + 2 * t + h,
                                        slot == 1 and k == 0, slot == 2 and k == 1)
                    if t == 1:
                        m.then_inc(used[slot], 1)
                    if t == 1 and slot == 1:
                        xt_tile_pe(pe, 2, 0, mixed)
                if t == 0:
                    m.then_inc(branch_tile0, 1)
            first_strip(pe, 2, mixed, T_WOUT1, STRIP, turned=True)
            last_strip(pe, T_WOUT1 + 1, 2, lambda: xt_tile_pe(pe, 3, 0, normed))

            def step(s, par, first=False):
                strip(pe, mlp_up(s), pair(par), between=lambda: hid_tr_pe(pe, s - 1, 1 - par, False))
                down(pe, T_MLP + 2 * s, MLP_DOWN, s - 1, first, False)
            first_strip(pe, 3, normed, T_MLP, STRIP, at=6, turned=True)
            step(1, 1, True)
            with pe.Fori(2, MLP_S, 2) as s:
                step(s, 0)
                step(s + 1, 1)
            last_down(pe, T_LAYER - 1, MLP_DOWN, MLP_S - 1, 1, False)
            with pe.Fori(0, LAYERS) as l:
                t, g, n = T_LAYER + L_TRIPLES * l, MLP_S + 2 * FFN_S * l, XT1 * (l + 1)
                base, qk = UNITS * (l + 1), QK1_BANKS + QK2_BANKS * l
                ffn_pe(pe, t, g, 2 * l, n, True)
                out0 = 2 * (S1 + S2 * l)

                def turn(events, heads):
                    pe.wait_ge(roped, 4 * (l + 1) + heads)
                    pe.wait_ge(roped1, 4 * l + heads)
                    qk_pe(pe, qk, events, 4, 3, qk_src2, QK2_TILES)

                turns = {2: ((0, 1), 1), 3: ((2, 3), 2), 4: ((4, 5, 6), 4)}
                for j in range(S2):
                    if j >= 2:
                        pe.wait_ge(proj_out, out0 + 2 * (j - 1))
                    if j == 0:
                        first_strip(pe, n + 1, xres, t + L_PROJ, STRIP, at=6)
                        continue
                    strip(pe, t + L_PROJ + j, pair(j % 2), PROJ2[j][1],
                          between=(lambda: turn(*turns[j])) if j in turns else None, at=5 if j == S2 - 1 else 2)
                pe.wait_ge(qk_out, qk + QK2_BANKS)
                for i in range(UNITS + 2):
                    if i >= 2:
                        turn_probs(pe, False, base, i - 2)
                    if i == 1:
                        pe.wait_ge(proj_out, out0 + 2 * S2)
                    if i < UNITS:
                        scores(pe, False, base, i)
                    if i >= 2:
                        outputs(pe, False, base, i - 2)
                first_strip(pe, n + 2, heads_out, t + L_WOUT, STRIP)
                last_strip(pe, t + L_WOUT + 1, 2)
                ffn_pe(pe, t + L_FFN2, g + FFN_S, 2 * l + 1, n + 3, False, l)
                xt_tile_pe(pe, n + 4, 0, xres)


_INS = ['x', 'positions', 'ln1_g', 'w_in', 'q_norm_a', 'k_norm_a', 'q_norm_b', 'k_norm_b', 'sinks', 'w_branch_a',
        'w_branch_b', 'w_out', 'ln2_g', 'w_up', 'w_down', 'positions_2', 'w_in_2', 'w_out_2', 'diff_lambda_2',
        'diff_subln_g_2', 'swa_sink_2', 'ffn1_w_in_2', 'ffn1_w_out_2', 'ffn2_w_in_2', 'ffn2_w_out_2', 'ln_g_2',
        'ln_b_2']


def kernel(**inputs):
    import concourse.bacc as _bacc
    from concourse.bass_utils import run_bass_kernel_spmd as _run

    nc = _bacc.Bacc("TRN2", target_bir_lowering=False, num_devices=1)
    arrays, args = {}, []
    for name in _INS:
        a = np.ascontiguousarray(inputs[name])
        arrays[f"in_{name}_dram"] = a
        args.append(nc.dram_tensor(f"in_{name}_dram", a.shape, mybir.dt.from_np(a.dtype), kind="ExternalInput").ap())
    args.append(nc.dram_tensor("out_0_dram", (1, TOK, DM), F32, kind="ExternalOutput").ap())
    build(nc, *args)
    r = _run(nc, [arrays], core_ids=[0])
    return r.results[0]["out_0_dram"]
```
